# Optimizing a Trainium2 kernel written in Bass

```python
import jax, jax.numpy as jnp
from jax import lax
import numpy as np

D_MODEL = 2048
BATCH = 1
SEQ = 256
DEPTH = 1

HEAD_DIM = 128
N_MIX_HEADS = D_MODEL // HEAD_DIM
N_HEADS_A = 4
N_HEADS_B = 6
N_HEADS_C = 6
DILATED_PATTERNS = ((128, 1), (512, 4), (2048, 16))
C_HEADS_PER_PATTERN = N_HEADS_C // len(DILATED_PATTERNS)
OUT_WIDTH = (N_HEADS_A + N_HEADS_B + C_HEADS_PER_PATTERN) * HEAD_DIM
MOBA_BLOCK = 256
MOBA_TOPK = 3
MOBA_Q_CHUNK = 64
SB_Q_BLOCK = 128
ROPE_THETA = 10000.0
MEM_LEN = 256
CROSS_HEADS = 4
CROSS_HEAD_DIM = 128
D_FF = 4 * D_MODEL
RMS_EPS = 1e-6
NEG_INF = -1e30

kernel_name = "hybrid_moba_stickbreak_dilated_block"

def rms_norm(x, g):
    x32 = x.astype(jnp.float32)
    y = x32 * lax.rsqrt(jnp.mean(x32 * x32, axis=-1, keepdims=True) + RMS_EPS)
    return (y * g.astype(jnp.float32)).astype(x.dtype)

def rope_tables(seq_len):
    inv_freq = 1.0 / (ROPE_THETA ** (jnp.arange(0, HEAD_DIM, 2, dtype=jnp.float32) / HEAD_DIM))
    ang = jnp.arange(seq_len, dtype=jnp.float32)[:, None] * inv_freq[None, :]
    return jnp.cos(ang), jnp.sin(ang)

def apply_rope(x, cos, sin):
    x32 = x.astype(jnp.float32)
    x1, x2 = jnp.split(x32, 2, axis=-1)
    return jnp.concatenate([x1 * cos - x2 * sin, x2 * cos + x1 * sin], axis=-1).astype(x.dtype)

def heads_to_channels(o):
    b, h, s, d = o.shape
    return jnp.transpose(o, (0, 2, 1, 3)).reshape(b, s, h * d)

def moba_attention(q, k, v):
    bsz, nh, seq, dh = q.shape
    scale = dh ** -0.5
    n_blk = -(-seq // MOBA_BLOCK)
    pad = ((0, 0), (0, 0), (0, n_blk * MOBA_BLOCK - seq), (0, 0))
    k_blk = jnp.pad(k, pad).reshape(bsz, nh, n_blk, MOBA_BLOCK, dh)
    v_blk = jnp.pad(v, pad).reshape(bsz, nh, n_blk, MOBA_BLOCK, dh)
    k_mean = jnp.mean(k_blk.astype(jnp.float32), axis=3)
    n_sel = min(MOBA_TOPK, n_blk - 1)
    n_chunk = seq // MOBA_Q_CHUNK
    q_chunks = jnp.moveaxis(q.reshape(bsz, nh, n_chunk, MOBA_Q_CHUNK, dh), 2, 0)
    starts = jnp.arange(n_chunk, dtype=jnp.int32) * MOBA_Q_CHUNK
    b_idx = jnp.arange(bsz)[:, None, None, None]
    h_idx = jnp.arange(nh)[None, :, None, None]
    blk_ids = jnp.arange(n_blk)
    in_blk = jnp.arange(MOBA_BLOCK)
    q_off = jnp.arange(MOBA_Q_CHUNK)

    def one_chunk(args):
        qc, start = args
        own = start // MOBA_BLOCK
        t_q = start + q_off
        k_own = lax.dynamic_index_in_dim(k_blk, own, axis=2, keepdims=False)
        v_own = lax.dynamic_index_in_dim(v_blk, own, axis=2, keepdims=False)
        s_own = jnp.einsum('bhqd,bhnd->bhqn', qc, k_own, preferred_element_type=jnp.float32) * scale
        causal = (own * MOBA_BLOCK + in_blk)[None, :] <= t_q[:, None]
        s_own = jnp.where(causal, s_own, NEG_INF)
        if n_sel == 0:
            p = jax.nn.softmax(s_own, axis=-1).astype(v.dtype)
            return jnp.einsum('bhqn,bhnd->bhqd', p, v_own)
        gate = jnp.einsum('bhqd,bhjd->bhqj', qc.astype(jnp.float32), k_mean)
        gate = jnp.where(blk_ids < own, gate, NEG_INF)
        _, sel = lax.top_k(gate, n_sel)
        sel_valid = sel < own
        k_sel = k_blk[b_idx, h_idx, sel]
        v_sel = v_blk[b_idx, h_idx, sel]
        s_sel = jnp.einsum('bhqd,bhqknd->bhqkn', qc, k_sel, preferred_element_type=jnp.float32) * scale
        s_sel = jnp.where(sel_valid[..., None], s_sel, NEG_INF)
        width = n_sel * MOBA_BLOCK
        scores = jnp.concatenate([s_sel.reshape(bsz, nh, MOBA_Q_CHUNK, width), s_own], axis=-1)
        p = jax.nn.softmax(scores, axis=-1).astype(v.dtype)
        p_sel = p[..., :width].reshape(bsz, nh, MOBA_Q_CHUNK, n_sel, MOBA_BLOCK)
        p_own = p[..., width:]
        return (jnp.einsum('bhqkn,bhqknd->bhqd', p_sel, v_sel)
                + jnp.einsum('bhqn,bhnd->bhqd', p_own, v_own))

    out = lax.map(one_chunk, (q_chunks, starts))
    return jnp.moveaxis(out, 0, 2).reshape(bsz, nh, seq, dh)

def stick_breaking_attention(q, k, v):
    bsz, nh, seq, dh = q.shape
    scale = dh ** -0.5
    outs = []
    for i in range(seq // SB_Q_BLOCK):
        lo, hi = i * SB_Q_BLOCK, (i + 1) * SB_Q_BLOCK
        z = jnp.einsum('bhqd,bhkd->bhqk', q[:, :, lo:hi], k[:, :, :hi],
                       preferred_element_type=jnp.float32) * scale
        past = jnp.arange(hi)[None, :] < jnp.arange(lo, hi)[:, None]
        log_keep = jnp.where(past, jax.nn.log_sigmoid(-z), 0.0)
        log_stick = lax.cumsum(log_keep, axis=3, reverse=True) - log_keep
        w = jnp.where(past, jnp.exp(jax.nn.log_sigmoid(z) + log_stick), 0.0)
        outs.append(jnp.einsum('bhqk,bhkd->bhqd', w.astype(v.dtype), v[:, :, :hi]))
    return jnp.concatenate(outs, axis=2)

def banded_causal_attention(q, k, v, steps):
    bsz, nh, n, dh = q.shape
    scale = dh ** -0.5
    blk = steps
    n_blk = -(-n // blk)
    pad = ((0, 0), (0, 0), (0, n_blk * blk - n), (0, 0))
    qb = jnp.pad(q, pad).reshape(bsz, nh, n_blk, blk, dh)
    kb = jnp.pad(k, pad).reshape(bsz, nh, n_blk, blk, dh)
    vb = jnp.pad(v, pad).reshape(bsz, nh, n_blk, blk, dh)

    def with_prev(xb):
        prev = jnp.concatenate([jnp.zeros_like(xb[:, :, :1]), xb[:, :, :-1]], axis=2)
        return jnp.concatenate([prev, xb], axis=3)

    kk, vv = with_prev(kb), with_prev(vb)
    s = jnp.einsum('bhnqd,bhnkd->bhnqk', qb, kk, preferred_element_type=jnp.float32) * scale
    qi = jnp.arange(blk)[:, None]
    kj = jnp.arange(2 * blk)[None, :]
    dist = qi + blk - kj
    key_pos = jnp.arange(n_blk)[:, None, None] * blk - blk + kj[None]
    mask = (dist >= 0) & (dist <= steps) & (key_pos >= 0)
    s = jnp.where(mask, s, NEG_INF)
    lse = jax.nn.logsumexp(s, axis=-1)
    p = jnp.exp(s - lse[..., None]).astype(v.dtype)
    out = jnp.einsum('bhnqk,bhnkd->bhnqd', p, vv).reshape(bsz, nh, n_blk * blk, dh)[:, :, :n]
    return out, lse.reshape(bsz, nh, n_blk * blk)[:, :, :n]

def dilated_attention(q, k, v, window, dilation):
    bsz, nh, seq, dh = q.shape
    sub = seq // dilation

    def split(x):
        return jnp.transpose(x.reshape(bsz, nh, sub, dilation, dh), (0, 1, 3, 2, 4)).reshape(bsz, nh * dilation, sub, dh)

    out, lse = banded_causal_attention(split(q), split(k), split(v), window // dilation)
    out = jnp.transpose(out.reshape(bsz, nh, dilation, sub, dh), (0, 1, 3, 2, 4)).reshape(bsz, nh, seq, dh)
    lse = jnp.transpose(lse.reshape(bsz, nh, dilation, sub), (0, 1, 3, 2)).reshape(bsz, nh, seq)
    return out, lse

def dilated_mixture(q, k, v):
    outs, lses = [], []
    for g, (window, dilation) in enumerate(DILATED_PATTERNS):
        sl = slice(g * C_HEADS_PER_PATTERN, (g + 1) * C_HEADS_PER_PATTERN)
        o, l = dilated_attention(q[:, sl], k[:, sl], v[:, sl], window, dilation)
        outs.append(o)
        lses.append(l)
    alpha = jax.nn.softmax(jnp.stack(lses, axis=0), axis=0)
    mixed = jnp.sum(alpha[..., None] * jnp.stack(outs, axis=0).astype(jnp.float32), axis=0)
    return mixed.astype(v.dtype)

def cross_attention(h, mem_n, w_q, w_kv, w_o):
    bsz, seq, _ = h.shape
    m = mem_n.shape[1]
    q = jnp.einsum('bsd,de->bse', h, w_q).reshape(bsz, seq, CROSS_HEADS, CROSS_HEAD_DIM)
    kv = jnp.einsum('bmd,de->bme', mem_n, w_kv).reshape(bsz, m, 2, CROSS_HEADS, CROSS_HEAD_DIM)
    s = jnp.einsum('bshd,bmhd->bhsm', q, kv[:, :, 0], preferred_element_type=jnp.float32) * CROSS_HEAD_DIM ** -0.5
    p = jax.nn.softmax(s, axis=-1).astype(h.dtype)
    o = jnp.einsum('bhsm,bmhd->bshd', p, kv[:, :, 1]).reshape(bsz, seq, CROSS_HEADS * CROSS_HEAD_DIM)
    return jnp.einsum('bse,ed->bsd', o, w_o)

def setup_inputs(seed: int = 0) -> dict:
    key = jax.random.key(seed)
    ks = jax.random.split(key, 17)
    f32 = jnp.float32

    def nrm(k, shape, scale):
        return jax.random.normal(k, shape, f32) * scale

    def gain(k, shape):
        return 1.0 + 0.02 * jax.random.normal(k, shape, f32)

    cw = CROSS_HEADS * CROSS_HEAD_DIM
    return {
        "x": nrm(ks[0], (BATCH, SEQ, D_MODEL), 1.0),
        "mem": nrm(ks[1], (BATCH, MEM_LEN, D_MODEL), 1.0),
        "g_mix": gain(ks[2], (DEPTH, D_MODEL)),
        "w_in": nrm(ks[3], (DEPTH, D_MODEL, 3 * N_MIX_HEADS * HEAD_DIM), D_MODEL ** -0.5),
        "g_out_a": gain(ks[4], (DEPTH, N_HEADS_A * HEAD_DIM)),
        "g_out_b": gain(ks[5], (DEPTH, N_HEADS_B * HEAD_DIM)),
        "g_out_c": gain(ks[6], (DEPTH, C_HEADS_PER_PATTERN * HEAD_DIM)),
        "w_out": nrm(ks[7], (DEPTH, OUT_WIDTH, D_MODEL), OUT_WIDTH ** -0.5),
        "g_cross": gain(ks[8], (DEPTH, D_MODEL)),
        "g_mem": gain(ks[9], (D_MODEL,)),
        "w_cq": nrm(ks[10], (DEPTH, D_MODEL, cw), D_MODEL ** -0.5),
        "w_ckv": nrm(ks[11], (DEPTH, D_MODEL, 2 * cw), D_MODEL ** -0.5),
        "w_co": nrm(ks[12], (DEPTH, cw, D_MODEL), cw ** -0.5),
        "g_mlp": gain(ks[13], (DEPTH, D_MODEL)),
        "w_up": nrm(ks[14], (DEPTH, D_MODEL, D_FF), D_MODEL ** -0.5),
        "w_down": nrm(ks[15], (DEPTH, D_FF, D_MODEL), D_FF ** -0.5),
        "g_final": gain(ks[16], (D_MODEL,)),
    }

def reference(x, mem, g_mix, w_in, g_out_a, g_out_b, g_out_c, w_out, g_cross, g_mem,
              w_cq, w_ckv, w_co, g_mlp, w_up, w_down, g_final):
    bsz, seq, _ = x.shape
    cos, sin = rope_tables(seq)
    mem_n = rms_norm(mem, g_mem)
    ha, hb = N_HEADS_A, N_HEADS_A + N_HEADS_B
    for l in range(DEPTH):
        h = rms_norm(x, g_mix[l])
        qkv = jnp.einsum('bsd,de->bse', h, w_in[l]).reshape(bsz, seq, 3, N_MIX_HEADS, HEAD_DIM)
        q = jnp.transpose(qkv[:, :, 0], (0, 2, 1, 3))
        k = jnp.transpose(qkv[:, :, 1], (0, 2, 1, 3))
        v = jnp.transpose(qkv[:, :, 2], (0, 2, 1, 3))
        o_a = moba_attention(apply_rope(q[:, :ha], cos, sin), apply_rope(k[:, :ha], cos, sin), v[:, :ha])
        o_b = stick_breaking_attention(q[:, ha:hb], k[:, ha:hb], v[:, ha:hb])
        o_c = dilated_mixture(apply_rope(q[:, hb:], cos, sin), apply_rope(k[:, hb:], cos, sin), v[:, hb:])
        merged = jnp.concatenate([
            rms_norm(heads_to_channels(o_a), g_out_a[l]),
            rms_norm(heads_to_channels(o_b), g_out_b[l]),
            rms_norm(heads_to_channels(o_c), g_out_c[l]),
        ], axis=-1)
        x = x + jnp.einsum('bse,ed->bsd', merged, w_out[l])
        x = x + cross_attention(rms_norm(x, g_cross[l]), mem_n, w_cq[l], w_ckv[l], w_co[l])
        u = jnp.einsum('bsd,df->bsf', rms_norm(x, g_mlp[l]), w_up[l])
        x = x + jnp.einsum('bsf,fd->bsd', jnp.square(jax.nn.relu(u)), w_down[l])
    return rms_norm(x, g_final)


_drawn_inputs = setup_inputs


def setup_inputs(seed=0):
    import zlib

    import numpy as np

    out = dict(_drawn_inputs(seed))
    spreads = {}
    factors = {'g_out_a': 6.711,
     'g_out_b': 5.355,
     'g_out_c': 8.0,
     'g_cross': 8.0,
     'g_mem': 8.0,
     'g_mlp': 10.331,
     'g_final': 8.506}
    for name, (base, spread) in spreads.items():
        noise = np.random.default_rng([zlib.crc32(name.encode()), seed]).standard_normal(out[name].shape)
        drawn = base * np.exp(spread * noise) if base else spread * noise
        out[name] = __import__('jax').numpy.asarray(drawn.astype(out[name].dtype))
    for name, factor in factors.items():
        out[name] = (out[name] * factor).astype(out[name].dtype)
    return out
```

```python
from contextlib import ExitStack

import concourse.bass as bass
import numpy as np
from concourse import mybir

D = 2048
T = 256
P = 128
HEADS_A, HEADS_B, HEADS_C = 4, 6, 6
PATTERNS = ((128, 1), (512, 4), (2048, 16))
HEADS = HEADS_A + HEADS_B + HEADS_C
CROSS = 4
D_FF = 4 * D
EPS = 1e-6
SCALE = P ** -0.5
NEG = -1e30
THETA = 10000.0

KT = D // P
QT = T // P
MIX_C = HEADS_C // len(PATTERNS)
MIX = HEADS_A + HEADS_B + MIX_C
QUARTER = D_FF // 4 // P
CHUNK = KT * P
HALF = CHUNK // 2
CAUSAL = P + T

GROUP_V = 4
JOB_V = 0
JOB_B = JOB_V + HEADS * P // 512 * GROUP_V
JOB_C = JOB_B + 2 * HEADS_B
JOB_A = JOB_C + 2 * HEADS_C
JOB_MK = JOB_A + 2 * HEADS_A
JOB_MV = JOB_MK + CROSS
JOB_OUT = JOB_MV + GROUP_V
JOB_CQ = JOB_OUT + KT
JOB_CO = JOB_CQ + CROSS
JOB_MLP = JOB_CO + CROSS
JOBS = JOB_MLP + 4 * 2 * QUARTER

OUT_B = 2 * (HEADS * P // 512)
OUT_C = OUT_B + 2 * HEADS_B
OUT_A = OUT_C + 2 * HEADS_C
OUT_MK = OUT_A + 2 * HEADS_A
OUT_MV = OUT_MK + CROSS
OUT_OUT = OUT_MV + QT
OUT_CQ = OUT_OUT + KT
OUT_CO = OUT_CQ + 2 * CROSS
OUT_MLP = OUT_CO + KT
BANKS = 4

G_MIX, G_OUT, G_CROSS = 0, KT, KT + MIX
G_MEM, G_MLP, G_FINAL = G_CROSS + KT, G_CROSS + 2 * KT, G_CROSS + 3 * KT
GAINS = G_FINAL + KT

SLOT_B, SLOT_C = 0, 4 * HEADS_A
SLOTS = SLOT_C + 2 * HEADS_C
SLOT_MK, SLOT_MV, SLOT_OA, SLOT_CQ = SLOT_C, SLOT_C + CROSS, SLOT_C + 2 * CROSS, 0


def slot_a(n):
    return n * 2 + 1


def slot_o(n):
    return n * 2


def build(nc, x_in, mem_in, wqk_in, wv_in, wmk_in, wmv_in, wout_in, wcq_in, wco_in, wup_in,
          wdown_in, gains_in, rope_in, masks_in, square_in, out):
    F32, F32R = mybir.dt.float32, mybir.dt.float32r
    ACT, ALU, AX = mybir.ActivationFunctionType, mybir.AluOpType, mybir.AxisListType

    with ExitStack() as ctx:
        def sb(name, shape, dt=F32):
            return ctx.enter_context(nc.sbuf_tensor(name, shape, dt))

        def sem(name):
            return ctx.enter_context(nc.semaphore(name))

        x = sb("x", [P, KT, T])
        part_a = sb("part_a", [P, KT, 2, T], F32R)
        part_b = sb("part_b", [P, KT, 2, T], F32R)
        staged = sb("staged", [P, 4, CHUNK])
        w_high = sb("w_high", [P, 2, CHUNK], F32R)
        w_low = sb("w_low", [P, 2, CHUNK], F32R)
        qk = sb("qk", [P, SLOTS, T])
        values = sb("values", [P, QT, HEADS * P])
        masks = sb("masks", [P, 2 + len(PATTERNS), CAUSAL])
        square = sb("square", [P, 3, P])
        gains = sb("gains", [P, GAINS])
        rope = sb("rope", [P, 2, T])
        spare = sb("spare", [P, 2, T])
        acc = sb("acc", [P, T])
        squares = sb("squares", [P, T])
        factor = sb("factor", [P, 3, T + QT])
        peak, total = sb("peak", [P, 4]), sb("total", [P, 4])
        eps = sb("eps", [P, 1])
        ident, ones, below = square[:, 0, :], square[:, 1, :], square[:, 2, :]
        MASK_A, MASK_B, MASK_C = 0, 1, 2

        flat = x[:, :, :].rearrange("p t n -> p (t n)")
        score = [flat[:, h * CAUSAL:(h + 1) * CAUSAL] for h in range(2)]
        soft = [flat[:, (2 + h) * CAUSAL:(3 + h) * CAUSAL] for h in range(2)]
        weight = [flat[:, (4 + h) * CAUSAL:(5 + h) * CAUSAL] for h in range(2)]
        scores_c = flat[:, 0:3 * CAUSAL].rearrange("p (g n) -> p g n", g=3)
        weights_c = flat[:, 3 * CAUSAL:6 * CAUSAL].rearrange("p (g n) -> p g n", g=3)
        held = 6 * CAUSAL
        held_qk = [flat[:, held + 512 * h:held + 512 * h + T] for h in range(3)]
        held_v = [flat[:, held + 512 * h + T:held + 512 * (h + 1)].rearrange("p (t n) -> p t n", t=QT)
                  for h in range(3)]
        flat_v = values[:, :, :].rearrange("p t n -> p (t n)")
        cross_p = [flat_v[:, h * 512:(h + 1) * 512] for h in range(2)]
        cross_w = [flat_v[:, (2 + h) * 512:(3 + h) * 512] for h in range(2)]
        cross_peak = flat_v[:, 2048:2056]
        cross_bias = flat_v[:, 2056:2064]
        cross_total = flat_v[:, 2064:2072]
        mem_raw = qk[:, 0:KT, :]
        mem_v = qk[:, SLOT_MV:SLOT_MV + CROSS, :].rearrange("p s n -> p (s n)").rearrange(
            "p (t n) -> p t n", t=QT)

        bank = [ctx.enter_context(nc.psum_tensor(f"bank{n}", [P, 512], F32)) for n in range(BANKS)]
        extra = [ctx.enter_context(nc.psum_tensor(f"extra{n}", [P, 512], F32)) for n in range(4)]

        landed = [sem(f"landed{n}") for n in range(4)]
        high_ready = sem("high_ready")
        low_ready = sem("low_ready")
        half_done = sem("half_done")
        taken = sem("taken")
        x_landed = [sem(f"x_landed{n}") for n in range(4)]
        gains_landed, const_landed, mem_landed, x_again = (
            sem("gains_landed"), sem("const_landed"), sem("mem_landed"), sem("x_again"))
        in_high, in_low, mem_high, mem_low = sem("in_high"), sem("in_low"), sem("mem_high"), sem("mem_low")
        acc_clear, sq_made, acc_made = sem("acc_clear"), sem("sq_made"), sem("acc_made")
        sum_ready, log_ready, factor_ready = sem("sum_ready"), sem("log_ready"), sem("factor_ready")
        rope_ready, v_scaled = sem("rope_ready"), sem("v_scaled")
        turned, rope_made = sem("turned"), sem("rope_made")
        held_ready, s_ready, t_ready, o_ready, o_taken = (
            sem("held_ready"), sem("s_ready"), sem("t_ready"), sem("o_ready"), sem("o_taken"))
        z_ready, abs_ready, exp_ready, ln_ready, soft_ready, logw_ready, w_ready = (
            sem("z_ready"), sem("abs_ready"), sem("exp_ready"), sem("ln_ready"), sem("soft_ready"),
            sem("logw_ready"), sem("w_ready"))
        masked_c, peak_c, exp_c, inv_c, prob_c, w_c = (
            sem(n) for n in ("masked_c", "peak_c", "exp_c", "inv_c", "prob_c", "w_c"))
        masked_a, peak_a, exp_a, inv_a, prob_a, w_a = (
            sem(n) for n in ("masked_a", "peak_a", "exp_a", "inv_a", "prob_a", "w_a"))
        merged, merged_high, merged_low = sem("merged"), sem("merged_high"), sem("merged_low")
        x1_high, x1_low, x2_high, x2_low = sem("x1_high"), sem("x1_low"), sem("x2_high"), sem("x2_low")
        cross_s, cross_max, cross_neg, cross_exp, cross_inv, cross_prob = (
            sem(n) for n in ("cross_s", "cross_max", "cross_neg", "cross_exp", "cross_inv", "cross_prob"))
        cross_t, cross_wt, cross_o, cross_high, cross_low = (
            sem(n) for n in ("cross_t", "cross_wt", "cross_o", "cross_high", "cross_low"))
        act_ready, sq_ready, hid_high, hid_low = (
            sem("act_ready"), sem("sq_ready"), sem("hid_high"), sem("hid_low"))
        y_ready, stored = sem("y_ready"), sem("stored")

        block = ctx.enter_context(nc.Block())

        def f32(ap):
            return ap.bitcast(F32)

        def by(i, n=4):
            return lambda k: i * (n * k)

        def none(k):
            return 0

        @block.sync
        def _(sp):
            def load(src, off, job, cols=CHUNK):
                if job >= 4:
                    sp.wait_ge(low_ready, off(2) + (2 * job - 6))
                sp.dma_start(staged[:, job % 4, 0:cols], src).then_inc(landed[job % 4], 16)

            def stream(src, job, count, cols=CHUNK):
                with sp.Fori(0, count // 4) as i:
                    for s in range(4):
                        load(src[i * 4 + s, :, 0:cols], by(i), job + s, cols)

            for part in range(4):
                sp.dma_start(x[:, 4 * part:4 * part + 4, :],
                             x_in[:, 4 * part:4 * part + 4, :]).then_inc(x_landed[part], 16)
                if part < 2:
                    load(wv_in[part, :, :], none, part)
            for s in range(2, 4):
                load(wv_in[s, :, :], none, s)
            sp.dma_start(mem_raw, mem_in).then_inc(mem_landed, 16)
            for s in range(4):
                load(wv_in[4 + s, :, :], none, 4 + s)
            with sp.Fori(0, 2) as i:
                for s in range(4):
                    load(wv_in[i * 4 + (8 + s), :, :], by(i), 8 + s)
            stream(wqk_in, JOB_B, 2 * HEADS)
            stream(wmk_in, JOB_MK, CROSS)
            stream(wmv_in, JOB_MV, GROUP_V)
            sp.wait_ge(o_ready, 7)
            sp.dma_start(x[:, :, :], x_in).then_inc(x_again, 16)
            stream(wout_in, JOB_OUT, KT, MIX * P)
            stream(wcq_in, JOB_CQ, CROSS)
            stream(wco_in, JOB_CO, CROSS)
            with sp.Fori(0, 4) as q:
                for part, src in enumerate((wup_in, wdown_in)):
                    with sp.Fori(0, QUARTER // 4) as i:
                        for s in range(4):
                            load(src[q * 16 + i * 4 + s, :, :],
                                 lambda k: q * (32 * k) + i * (4 * k), JOB_MLP + 16 * part + s)
            for t in range(KT):
                sp.wait_ge(y_ready, t + 1)
                sp.dma_start(out[:, t, :], x[:, t, :]).then_inc(stored, 16)
            sp.wait_ge(stored, 16 * KT)

        SUMMED = [0]
        for tiles in (KT, KT, HEADS_B, MIX_C, HEADS_A, KT, KT, KT):
            SUMMED.append(SUMMED[-1] + tiles)
        N_X, N_MEM, N_B, N_C, N_A, N_X1, N_X2, N_LAST = range(8)
        F_X, F_MEM, F_B, F_C, F_A, F_X1, F_X2, F_LAST = 0, 1, 2, 0, 2, 1, 0, 1

        @block.gpsimd
        def _(pool):
            def clear(norm):
                if norm:
                    pool.wait_ge(sum_ready, norm)
                nc.gpsimd.memset(acc[:, :], 0.0).then_inc(acc_clear, 1)
                pool.wait_ge(acc_clear, norm + 1)

            def add_square(tile, norm, t, off=0):
                n = off + (SUMMED[norm] + t)
                pool.wait_ge(acc_made, n)
                nc.gpsimd.tensor_tensor(squares[:, :], tile, tile, ALU.mult).then_inc(sq_made, 1)
                pool.wait_ge(sq_made, n + 1)
                nc.gpsimd.tensor_tensor(acc[:, :], acc[:, :], squares[:, :], ALU.add).then_inc(acc_made, 1)

            def hold(it, pairs):
                pool.wait_ge(o_ready, it)
                for to, at in pairs:
                    nc.gpsimd.tensor_copy(to, at).then_inc(held_ready, 1)

            nc.gpsimd.memset(eps[:, :], EPS)
            clear(N_X)
            for t in range(KT):
                if t % 4 == 0:
                    pool.wait_ge(x_landed[t // 4], 16)
                add_square(x[:, t, :], N_X, t)
            clear(N_MEM)
            pool.wait_ge(mem_landed, 16)
            for t in range(KT):
                add_square(mem_raw[:, t, :], N_MEM, t)

            pool.wait_ge(taken, BANKS + OUT_C)
            pool.wait_ge(v_scaled, 2)
            with pool.Fori(0, HEADS_B // 2) as i:
                hold(i, [(held_qk[h], qk[:, i * 4 + (SLOT_B + 2 * h + 1), :]) for h in range(2)]
                     + [(held_v[h], values[:, :, bass.ds(i * 256 + (HEADS_A + h) * P, P)])
                        for h in range(2)])
            clear(N_B)
            pool.wait_ge(o_taken, HEADS_B)
            for t in range(HEADS_B):
                add_square(qk[:, slot_o(t), :], N_B, t)
            pool.wait_ge(taken, BANKS + OUT_A)
            with pool.Fori(0, MIX_C) as i:
                hold(i + 3, [(held_qk[g], qk[:, i * 2 + (SLOT_C + 4 * g), :]) for g in range(3)]
                     + [(held_v[g], values[:, :, bass.ds(i * P + (HEADS_A + HEADS_B + 2 * g) * P, P)])
                        for g in range(3)])
            clear(N_C)
            pool.wait_ge(o_taken, HEADS_B + MIX_C)
            for t in range(MIX_C):
                add_square(qk[:, slot_o(HEADS_B + t), :], N_C, t)
            clear(N_A)
            for t in range(HEADS_A):
                pool.wait_ge(o_taken, HEADS_B + MIX_C + t + 1)
                add_square(qk[:, SLOT_OA + t, :], N_A, t)
            clear(N_X1)
            with pool.Fori(0, KT // 4) as i:
                for s in range(4):
                    pool.wait_ge(taken, i * 4 + (BANKS + OUT_OUT + s + 1))
                    add_square(x[:, i * 4 + s, :], N_X1, s, i * 4)
            clear(N_X2)
            for t in range(KT):
                pool.wait_ge(taken, BANKS + OUT_CO + t + 1)
                add_square(x[:, t, :], N_X2, t)
            clear(N_LAST)
            with pool.Fori(0, KT // 4) as i:
                for s in range(4):
                    pool.wait_ge(taken, i * 4 + (BANKS + OUT_MLP + 3 * 32 + 16 + s + 1))
                    add_square(x[:, i * 4 + s, :], N_LAST, s, i * 4)

        @block.scalar
        def _(act):
            nc.scalar.preload_act_table_set("natural_log_exp_and_others")
            act.dma_start(gains[:, :], gains_in).then_inc(gains_landed, 16)
            for to, src in ((square, square_in), (rope, rope_in), (masks, masks_in)):
                act.dma_start(to[:, :, :], src).then_inc(const_landed, 16)

            def split(off, job, half):
                if half == 0:
                    act.wait_ge(landed[job % 4], off(4) + 16 * (job // 4 + 1))
                if job >= 2:
                    act.wait_ge(half_done, off(2) + (2 * (job - 2) + half + 1))
                cols = slice(half * HALF, (half + 1) * HALF)
                nc.scalar.activation(w_high[:, job % 2, cols], staged[:, job % 4, cols],
                                     ACT.Copy).then_inc(high_ready, 1)

            def norm_factor(norm, width, src, slot, cols=T):
                act.wait_ge(sum_ready, norm + 1)
                nc.scalar.activation(factor[:, slot, 0:cols], src[:, 0:cols], ACT.Ln, bias=eps[:, :],
                                     scale=1.0 / width).then_inc(log_ready, 1)
                act.wait_ge(log_ready, norm + 1)
                nc.scalar.activation(factor[:, slot, 0:cols], factor[:, slot, 0:cols], ACT.Exp,
                                     scale=-0.5).then_inc(factor_ready, 1)

            def turn(off, job, n_turn, n_out):
                act.wait_ge(half_done, off(2) + (2 * job + 2))
                act.wait_ge(taken, off(1) + (BANKS + n_out))
                src = bank[job % 4]
                nc.scalar.activation(spare[0:64, 0, :], src[64:P, 0:T], ACT.Copy)
                nc.scalar.activation(spare[64:P, 0, :], src[0:64, 0:T], ACT.Copy).then_inc(turned, 1)

            act.wait_ge(gains_landed, 16)
            for t in range(KT):
                if t % 4 == 0:
                    act.wait_ge(x_landed[t // 4], 16)
                nc.scalar.activation(part_a[:, t, 0, :], x[:, t, :], ACT.Copy,
                                     scale=gains[:, G_MIX + t:G_MIX + t + 1]).then_inc(in_high, 1)
                if t in (3, 7):
                    for half in range(2):
                        split(none, t // 4, half)
            act.wait_ge(acc_clear, 1)
            act.wait_ge(mem_landed, 16)
            with act.Fori(0, 2) as i:
                for s in range(8):
                    split(by(i, 8), JOB_V + s + 2, 0)
                    nc.scalar.activation(part_b[:, i * 8 + s, 0, :], mem_raw[:, i * 8 + s, :], ACT.Copy,
                                         scale=gains[:, bass.ds(i * 8 + (G_MEM + s), 1)]).then_inc(mem_high, 1)
                    split(by(i, 8), JOB_V + s + 2, 1)
            norm_factor(N_X, D, extra[0], F_X, T + QT)
            norm_factor(N_MEM, D, extra[1], F_MEM, T + QT)
            act.wait_ge(taken, BANKS + OUT_B)
            nc.scalar.activation(values[:, 0, :], values[:, 0, :], ACT.Copy,
                                 scale=factor[:, F_X, T:T + 1]).then_inc(v_scaled, 1)
            with act.Fori(0, HEADS_B // 2) as i:
                for s in range(4):
                    split(by(i), JOB_B + s + 2, 0)
                    split(by(i), JOB_B + s + 2, 1)
            with act.Fori(0, HEADS_C // 2) as i:
                for s in range(4):
                    if s == 2:
                        for h in range(2):
                            act.wait_ge(logw_ready, i * 2 + (h + 1))
                            nc.scalar.activation(weight[h], score[h], ACT.Exp).then_inc(w_ready, 1)
                    if s == 3:
                        act.wait_ge(o_ready, i + 1)
                        for h in range(2):
                            nc.scalar.activation(qk[:, i * 4 + slot_o(h), :], extra[h][:, 0:T],
                                                 ACT.Copy).then_inc(o_taken, 1)
                    split(by(i), JOB_C + s + 2, 0)
                    turn(by(i), JOB_C + s, s, OUT_C + s)
                    if s == 0:
                        for h in range(2):
                            act.wait_ge(abs_ready, i * 2 + (h + 1))
                            nc.scalar.activation(soft[h], soft[h], ACT.Exp, scale=-1.0).then_inc(exp_ready, 1)
                        for h in range(2):
                            act.wait_ge(exp_ready, i * 2 + (h + 1))
                            nc.scalar.activation(soft[h], soft[h], ACT.Ln, bias=1.0).then_inc(ln_ready, 1)
                    split(by(i), JOB_C + s + 2, 1)
            with act.Fori(0, HEADS_A // 2) as i:
                for s in range(4):
                    if s == 2:
                        act.wait_ge(t_ready, i + 4)
                        for g in range(3):
                            nc.scalar.activation(weights_c[:, g, :], extra[(g + 3) % 4][:, 0:CAUSAL],
                                                 ACT.Copy).then_inc(w_c, 1)
                    if s == 3:
                        act.wait_ge(o_ready, i + 4)
                        nc.scalar.activation(qk[:, i * 2 + slot_o(HEADS_B), :], extra[2][:, 0:T],
                                             ACT.Copy).then_inc(o_taken, 1)
                    split(by(i), JOB_A + s + 2, 0)
                    turn(by(i), JOB_A + s, s, OUT_A + s)
                    if s == 0:
                        for t in range(QT):
                            cols = slice(0, P) if t == 0 else slice(P, CAUSAL)
                            act.wait_ge(peak_c, i * 2 + (t + 1))
                            nc.scalar.activation(scores_c[:, :, cols], scores_c[:, :, cols], ACT.Exp,
                                                 bias=peak[:, t:t + 1],
                                                 accum_out=total[:, t:t + 1]).then_inc(exp_c, 1)
                    split(by(i), JOB_A + s + 2, 1)
            norm_factor(N_B, HEADS_B * P, extra[3], F_B)
            for i in range(HEADS_A // 2):
                for s in range(4):
                    if s == 2:
                        act.wait_ge(t_ready, 6 + i)
                        for h in range(2):
                            nc.scalar.activation(weight[h], extra[2 + h][:, 0:CAUSAL], ACT.Copy).then_inc(w_a, 1)
                    if s == 3:
                        act.wait_ge(o_ready, 6 + i)
                        for h in range(2):
                            nc.scalar.activation(qk[:, SLOT_OA + 2 * i + h, :], extra[h][:, 0:T],
                                                 ACT.Copy).then_inc(o_taken, 1)
                    split(none, JOB_MK + 4 * i + s + 2, 0)
                    tile = 4 * i + s
                    act.wait_ge(merged, tile + 1)
                    nc.scalar.activation(part_a[:, tile, 0, :], spare[:, tile % 2, :], ACT.Copy).then_inc(merged_high, 1)
                    if s == 0:
                        for n in range(4):
                            h, cols = n // 2, slice(0, P) if n % 2 == 0 else slice(P, CAUSAL)
                            act.wait_ge(peak_a, 4 * i + n + 1)
                            nc.scalar.activation(score[h][:, cols], score[h][:, cols], ACT.Exp,
                                                 bias=peak[:, n:n + 1],
                                                 accum_out=total[:, n:n + 1]).then_inc(exp_a, 1)
                    split(none, JOB_MK + 4 * i + s + 2, 1)
                if i == 0:
                    norm_factor(N_C, MIX_C * P, extra[3], F_C)
            norm_factor(N_A, HEADS_A * P, extra[3], F_A)
            for tile in range(HEADS_B + MIX_C, MIX):
                act.wait_ge(merged, tile + 1)
                nc.scalar.activation(part_a[:, tile, 0, :], spare[:, tile % 2, :], ACT.Copy).then_inc(merged_high, 1)
            with act.Fori(0, KT // 4) as i:
                for s in range(4):
                    split(by(i), JOB_OUT + s + 2, 0)
                    act.wait_ge(taken, i * 4 + (BANKS + OUT_OUT + s + 1))
                    nc.scalar.activation(part_b[:, i * 4 + s, 0, :], x[:, i * 4 + s, :], ACT.Copy,
                                         scale=gains[:, bass.ds(i * 4 + (G_CROSS + s), 1)]).then_inc(x1_high, 1)
                    split(by(i), JOB_OUT + s + 2, 1)

            def cross_exps(h):
                for t in range(QT):
                    n = 2 * h + t
                    act.wait_ge(cross_neg, n + 1)
                    nc.scalar.activation(cross_p[h % 2][:, t * T:(t + 1) * T], extra[h % 2][:, t * T:(t + 1) * T],
                                         ACT.Exp, bias=cross_bias[:, n:n + 1], scale=SCALE,
                                         accum_out=cross_total[:, n:n + 1]).then_inc(cross_exp, 1)

            def cross_weights(h):
                act.wait_ge(cross_t, h + 1)
                nc.scalar.activation(cross_w[h % 2], extra[2 + h % 2][:, :], ACT.Copy).then_inc(cross_wt, 1)

            def cross_part(h):
                act.wait_ge(cross_o, h + 1)
                nc.scalar.activation(part_b[:, h, 0, :], bank[h][:, 0:T], ACT.Copy).then_inc(cross_high, 1)

            for s in range(4):
                split(none, JOB_CQ + s + 2, 0)
                if s == 0:
                    norm_factor(N_X1, D, extra[3], F_X1)
                if s >= 2:
                    cross_exps(s - 2)
                if s == 3:
                    cross_weights(0)
                split(none, JOB_CQ + s + 2, 1)
            cross_exps(2)
            cross_weights(1)
            cross_part(0)
            cross_exps(3)
            cross_weights(2)
            cross_part(1)
            cross_weights(3)
            cross_part(2)
            cross_part(3)
            for s in range(4):
                for half in range(2):
                    split(none, JOB_CO + s + 2, half)
                    for t in (4 * s + 2 * half, 4 * s + 2 * half + 1):
                        act.wait_ge(taken, BANKS + OUT_CO + t + 1)
                        nc.scalar.activation(part_a[:, t, 0, :], x[:, t, :], ACT.Copy,
                                             scale=gains[:, G_MLP + t:G_MLP + t + 1]).then_inc(x2_high, 1)
            norm_factor(N_X2, D, extra[3], F_X2)

            def mlp_quarter(q, last):
                with act.Fori(0, QUARTER // 4) as i:
                    for s in range(4):
                        n = q * 16 + i * 4 + s
                        split(lambda k: q * (32 * k) + i * (4 * k), JOB_MLP + s + 2, 0)
                        act.wait_ge(act_ready, n + 1)
                        nc.scalar.activation(spare[:, 1, :], spare[:, 0, :], ACT.Square).then_inc(sq_ready, 1)
                        act.wait_ge(sq_ready, n + 1)
                        nc.scalar.activation(part_b[:, i * 4 + s, 0, :], spare[:, 1, :], ACT.Copy).then_inc(hid_high, 1)
                        split(lambda k: q * (32 * k) + i * (4 * k), JOB_MLP + s + 2, 1)
                with act.Fori(0, KT // 4 - last) as i:
                    for s in range(4):
                        for half in range(2):
                            split(lambda k: q * (32 * k) + i * (4 * k), JOB_MLP + QUARTER + s + 2, half)
                if last:
                    for s in range(2):
                        for half in range(2):
                            split(none, JOBS - 4 + s + 2, half)

            with act.Fori(0, 3) as q:
                mlp_quarter(q, 0)
            mlp_quarter(3, 1)
            norm_factor(N_LAST, D, extra[3], F_LAST)

        @block.vector
        def _(dve):
            tt = nc.vector.tensor_tensor
            stt = nc.vector.scalar_tensor_tensor

            def split(off, job, half):
                dve.wait_ge(high_ready, off(2) + (2 * job + half + 1))
                cols = slice(half * HALF, (half + 1) * HALF)
                tt(w_low[:, job % 2, cols], staged[:, job % 4, cols], f32(w_high[:, job % 2, cols]),
                   ALU.subtract).then_inc(low_ready, 1)

            def done(off, job):
                dve.wait_ge(half_done, off(2) + (2 * job + 2))

            def roped(off, slot, n_turn, n_out, job):
                done(off, job)
                src = bank[job % 4]
                dve.wait_ge(turned, off(1) + (n_turn + 1))
                tt(spare[:, 1, :], src[:, 0:T], rope[:, 0, :], ALU.mult).then_inc(rope_made, 1)
                tt(spare[:, 0, :], spare[:, 0, :], rope[:, 1, :], ALU.mult).then_inc(rope_made, 1)
                dve.wait_ge(rope_made, off(2) + (2 * n_turn + 2))
                tt(slot, spare[:, 0, :], spare[:, 1, :], ALU.add).then_inc(taken, 1)

            dve.sem_inc(taken, BANKS)
            for t in range(KT):
                dve.wait_ge(in_high, t + 1)
                stt(part_a[:, t, 1, :], x[:, t, :], gains[:, G_MIX + t:G_MIX + t + 1],
                    f32(part_a[:, t, 0, :]), ALU.mult, ALU.subtract).then_inc(in_low, 1)
                if t in (3, 7):
                    for half in range(2):
                        split(none, t // 4, half)
            with dve.Fori(0, 2) as i:
                for s in range(8):
                    split(by(i, 8), JOB_V + s + 2, 0)
                    dve.wait_ge(mem_high, i * 8 + (s + 1))
                    stt(part_b[:, i * 8 + s, 1, :], mem_raw[:, i * 8 + s, :],
                        gains[:, bass.ds(i * 8 + (G_MEM + s), 1)], f32(part_b[:, i * 8 + s, 0, :]),
                        ALU.mult, ALU.subtract).then_inc(mem_low, 1)
                    if s % 4 == 3:
                        done(by(i, 8), JOB_V + s)
                        for t in range(QT):
                            nc.vector.tensor_copy(values[:, t, bass.ds(i * 1024 + s // 4 * 512, 512)],
                                                  bank[s // 4 * 2 + t][:, :]).then_inc(taken, 1)
                    split(by(i, 8), JOB_V + s + 2, 1)
            dve.wait_ge(const_landed, 16 * 3)
            dve.wait_ge(factor_ready, 2)
            dve.wait_ge(taken, BANKS + OUT_B)
            nc.vector.tensor_scalar(values[:, 1, :], values[:, 1, :], factor[:, F_X, T + 1:T + 2], None,
                                    ALU.mult).then_inc(v_scaled, 1)
            for n in range(2):
                tt(rope[:, n, :], rope[:, n, :], factor[:, F_X, 0:T], ALU.mult).then_inc(rope_ready, 1)
            dve.wait_ge(rope_ready, 2)
            with dve.Fori(0, HEADS_B // 2) as i:
                for s in range(4):
                    split(by(i), JOB_B + s + 2, 0)
                    done(by(i), JOB_B + s)
                    tt(qk[:, i * 4 + (SLOT_B + s), :], bank[s][:, 0:T], factor[:, F_X, 0:T],
                       ALU.mult).then_inc(taken, 1)
                    split(by(i), JOB_B + s + 2, 1)
            with dve.Fori(0, HEADS_C // 2) as i:
                for s in range(4):
                    if s == 1:
                        for h in range(2):
                            dve.wait_ge(ln_ready, i * 2 + (h + 1))
                            stt(soft[h], score[h], 0.0, soft[h], ALU.max, ALU.add).then_inc(soft_ready, 1)
                    if s == 2:
                        dve.wait_ge(t_ready, i + 1)
                        for h in range(2):
                            tt(score[h], score[h], extra[2 + h][:, 0:CAUSAL], ALU.subtract).then_inc(logw_ready, 1)
                    split(by(i), JOB_C + s + 2, 0)
                    roped(by(i), qk[:, i * 4 + (SLOT_C + s), :], s, OUT_C + s, JOB_C + s)
                    if s == 0:
                        dve.wait_ge(s_ready, i + 1)
                        for h in range(2):
                            stt(score[h], extra[h][:, 0:CAUSAL], SCALE, masks[:, MASK_B, :],
                                ALU.mult, ALU.add).then_inc(z_ready, 1)
                        for h in range(2):
                            dve.wait_ge(z_ready, i * 2 + (h + 1))
                            stt(soft[h], score[h], -1.0, score[h], ALU.mult, ALU.max).then_inc(abs_ready, 1)
                    split(by(i), JOB_C + s + 2, 1)
            with dve.Fori(0, HEADS_A // 2) as i:
                for s in range(4):
                    if s == 1:
                        dve.wait_ge(exp_c, i * 2 + 2)
                        nc.vector.reciprocal(total[:, 0:2], total[:, 0:2]).then_inc(inv_c, 1)
                        dve.wait_ge(inv_c, i + 1)
                        for t in range(QT):
                            cols = slice(0, P) if t == 0 else slice(P, CAUSAL)
                            nc.vector.tensor_scalar(scores_c[:, :, cols], scores_c[:, :, cols],
                                                    total[:, t:t + 1], None, ALU.mult).then_inc(prob_c, 1)
                    split(by(i), JOB_A + s + 2, 0)
                    roped(by(i), qk[:, i * 8 + slot_a(s), :], 2 * HEADS_C + s, OUT_A + s, JOB_A + s)
                    if s == 0:
                        dve.wait_ge(s_ready, i + 4)
                        for g in range(3):
                            stt(scores_c[:, g, :], extra[g][:, 0:CAUSAL], SCALE, masks[:, MASK_C + g, :],
                                ALU.mult, ALU.add).then_inc(masked_c, 1)
                        dve.wait_ge(masked_c, i * 3 + 3)
                        for t in range(QT):
                            cols = slice(0, P) if t == 0 else slice(P, CAUSAL)
                            nc.vector.tensor_reduce(peak[:, t:t + 1], scores_c[:, :, cols], AX.XY, ALU.max,
                                                    negate=True).then_inc(peak_c, 1)
                    split(by(i), JOB_A + s + 2, 1)

            def merge(tile):
                src = qk[:, slot_o(tile), :] if tile < HEADS_B + MIX_C else qk[:, SLOT_OA + tile - HEADS_B - MIX_C, :]
                norm, slot = ((N_B, F_B) if tile < HEADS_B else (N_C, F_C) if tile < HEADS_B + MIX_C
                              else (N_A, F_A))
                dve.wait_ge(factor_ready, norm + 1)
                dve.wait_ge(merged_low, tile - 1 if tile >= 2 else 0)
                stt(spare[:, tile % 2, :], src, gains[:, G_OUT + tile:G_OUT + tile + 1],
                    factor[:, slot, 0:T], ALU.mult, ALU.mult).then_inc(merged, 1)

            def merge_low(tile):
                dve.wait_ge(merged, tile + 1)
                dve.wait_ge(merged_high, tile + 1)
                tt(part_a[:, tile, 1, :], spare[:, tile % 2, :], f32(part_a[:, tile, 0, :]),
                   ALU.subtract).then_inc(merged_low, 1)

            dve.wait_ge(taken, BANKS + OUT_MK)
            for i in range(HEADS_A // 2):
                for s in range(4):
                    job = JOB_MK + 4 * i + s
                    if s == 1:
                        dve.wait_ge(exp_a, 4 * i + 4)
                        nc.vector.reciprocal(total[:, 0:4], total[:, 0:4]).then_inc(inv_a, 1)
                        dve.wait_ge(inv_a, i + 1)
                        for n in range(4):
                            h, cols = n // 2, slice(0, P) if n % 2 == 0 else slice(P, CAUSAL)
                            nc.vector.tensor_scalar(score[h][:, cols], score[h][:, cols],
                                                    total[:, n:n + 1], None, ALU.mult).then_inc(prob_a, 1)
                    merge(4 * i + s)
                    split(none, job + 2, 0)
                    merge_low(4 * i + s)
                    done(none, job)
                    if i == 0:
                        tt(qk[:, SLOT_MK + s, :], bank[s][:, 0:T], factor[:, F_MEM, 0:T],
                           ALU.mult).then_inc(taken, 1)
                    elif s == 3:
                        for t in range(QT):
                            nc.vector.tensor_scalar(mem_v[:, t, :], bank[t][:, :],
                                                    factor[:, F_MEM, T + t:T + t + 1], None,
                                                    ALU.mult).then_inc(taken, 1)
                    if s == 0:
                        dve.wait_ge(s_ready, 6 + i)
                        for h in range(2):
                            stt(score[h], extra[h][:, 0:CAUSAL], SCALE, masks[:, MASK_A, :],
                                ALU.mult, ALU.add).then_inc(masked_a, 1)
                        for n in range(4):
                            h, cols = n // 2, slice(0, P) if n % 2 == 0 else slice(P, CAUSAL)
                            dve.wait_ge(masked_a, 2 * i + h + 1)
                            nc.vector.tensor_reduce(peak[:, n:n + 1], score[h][:, cols], AX.X, ALU.max,
                                                    negate=True).then_inc(peak_a, 1)
                    split(none, job + 2, 1)
            for tile in range(HEADS_B + MIX_C, MIX):
                merge(tile)
                if tile > HEADS_B + MIX_C:
                    merge_low(tile - 1)
            merge_low(MIX - 1)

            dve.wait_ge(x_again, 16)
            with dve.Fori(0, KT // 4) as i:
                for s in range(4):
                    split(by(i), JOB_OUT + s + 2, 0)
                    done(by(i), JOB_OUT + s)
                    tt(x[:, i * 4 + s, :], x[:, i * 4 + s, :], bank[s][:, 0:T], ALU.add).then_inc(taken, 1)
                    dve.wait_ge(x1_high, i * 4 + (s + 1))
                    stt(part_b[:, i * 4 + s, 1, :], x[:, i * 4 + s, :],
                        gains[:, bass.ds(i * 4 + (G_CROSS + s), 1)], f32(part_b[:, i * 4 + s, 0, :]),
                        ALU.mult, ALU.subtract).then_inc(x1_low, 1)
                    split(by(i), JOB_OUT + s + 2, 1)

            def cross_peaks(h):
                dve.wait_ge(cross_s, h + 1)
                nc.vector.tensor_reduce(cross_peak[:, 2 * h:2 * h + 2],
                                        extra[h % 2][:, :].rearrange("p (t n) -> p t n", t=QT), AX.X,
                                        ALU.max).then_inc(cross_max, 1)
                dve.wait_ge(cross_max, h + 1)
                nc.vector.tensor_scalar(cross_bias[:, 2 * h:2 * h + 2], cross_peak[:, 2 * h:2 * h + 2],
                                        -SCALE, None, ALU.mult).then_inc(cross_neg, 2)

            def cross_probs(h):
                dve.wait_ge(cross_exp, 2 * h + 2)
                nc.vector.reciprocal(cross_total[:, 2 * h:2 * h + 2],
                                     cross_total[:, 2 * h:2 * h + 2]).then_inc(cross_inv, 1)
                dve.wait_ge(cross_inv, h + 1)
                for t in range(QT):
                    cols = slice(t * T, (t + 1) * T)
                    nc.vector.tensor_scalar(cross_p[h % 2][:, cols], cross_p[h % 2][:, cols],
                                            cross_total[:, 2 * h + t:2 * h + t + 1], None,
                                            ALU.mult).then_inc(cross_prob, 1)

            def cross_lows(h):
                dve.wait_ge(cross_high, h + 1)
                tt(part_b[:, h, 1, :], bank[h][:, 0:T], f32(part_b[:, h, 0, :]),
                   ALU.subtract).then_inc(taken, 1)

            for s in range(4):
                split(none, JOB_CQ + s + 2, 0)
                if s == 0:
                    dve.wait_ge(factor_ready, N_X1 + 1)
                if s >= 2:
                    cross_peaks(s - 2)
                if s == 3:
                    cross_probs(0)
                done(none, JOB_CQ + s)
                tt(qk[:, SLOT_CQ + s, :], bank[s][:, 0:T], factor[:, F_X1, 0:T], ALU.mult).then_inc(taken, 1)
                split(none, JOB_CQ + s + 2, 1)
            cross_peaks(2)
            cross_probs(1)
            cross_peaks(3)
            cross_probs(2)
            cross_lows(0)
            cross_probs(3)
            cross_lows(1)
            cross_lows(2)
            cross_lows(3)
            for s in range(4):
                for half in range(2):
                    split(none, JOB_CO + s + 2, half)
                    dve.wait_ge(half_done, 2 * (JOB_CO + s) + half + 1)
                    for t in (4 * s + 2 * half, 4 * s + 2 * half + 1):
                        tt(x[:, t, :], x[:, t, :], bank[t % 4][:, 0:T], ALU.add).then_inc(taken, 1)
                    for t in (4 * s + 2 * half, 4 * s + 2 * half + 1):
                        dve.wait_ge(x2_high, t + 1)
                        stt(part_a[:, t, 1, :], x[:, t, :], gains[:, G_MLP + t:G_MLP + t + 1],
                            f32(part_a[:, t, 0, :]), ALU.mult, ALU.subtract).then_inc(x2_low, 1)

            def mlp_quarter(q, last):
                with dve.Fori(0, QUARTER // 4) as i:
                    for s in range(4):
                        n = q * 16 + i * 4 + s
                        off = lambda k: q * (32 * k) + i * (4 * k)
                        split(off, JOB_MLP + s + 2, 0)
                        done(off, JOB_MLP + s)
                        dve.wait_ge(hid_high, n)
                        stt(spare[:, 0, :], bank[s][:, 0:T], 0.0, factor[:, F_X2, 0:T],
                            ALU.max, ALU.mult).then_inc(act_ready, 1)
                        dve.wait_ge(act_ready, n + 1)
                        dve.sem_inc(taken, 1)
                        dve.wait_ge(hid_high, n + 1)
                        tt(part_b[:, i * 4 + s, 1, :], spare[:, 1, :], f32(part_b[:, i * 4 + s, 0, :]),
                           ALU.subtract).then_inc(hid_low, 1)
                        split(off, JOB_MLP + s + 2, 1)

                def down(off, i, s):
                    done(off, JOB_MLP + QUARTER + s)
                    tt(x[:, i * 4 + s, :], x[:, i * 4 + s, :], bank[s][:, 0:T], ALU.add).then_inc(taken, 1)

                with dve.Fori(0, KT // 4 - last) as i:
                    for s in range(4):
                        off = lambda k: q * (32 * k) + i * (4 * k)
                        split(off, JOB_MLP + QUARTER + s + 2, 0)
                        down(off, i, s)
                        split(off, JOB_MLP + QUARTER + s + 2, 1)
                if last:
                    for s in range(4):
                        off = lambda k: 3 * (32 * k) + 3 * (4 * k)
                        if s < 2:
                            split(none, JOBS - 4 + s + 2, 0)
                        down(off, 3, s)
                        if s < 2:
                            split(none, JOBS - 4 + s + 2, 1)

            dve.wait_ge(factor_ready, N_X2 + 1)
            dve.wait_ge(merged_low, MIX)
            with dve.Fori(0, 3) as q:
                mlp_quarter(q, 0)
            mlp_quarter(3, 1)
            dve.wait_ge(factor_ready, N_LAST + 1)
            for t in range(KT):
                stt(x[:, t, :], x[:, t, :], gains[:, G_FINAL + t:G_FINAL + t + 1], factor[:, F_LAST, 0:T],
                    ALU.mult, ALU.mult).then_inc(y_ready, 1)

        @block.tensor
        def _(pe):
            mm = nc.tensor.matmul

            def half_job(off, job, half, out, part, tiles, count=8, total=KT, place=0):
                pe.wait_ge(low_ready, off(2) + (2 * job + half + 1))
                for n in range(count):
                    kt = tiles + n
                    cols = slice(half * HALF + (place + n) * P, half * HALF + (place + n + 1) * P)
                    high, low = w_high[:, job % 2, cols], w_low[:, job % 2, cols]
                    mm(out, high, part[:, kt, 0, :], start=kt == 0, stop=False)
                    mm(out, high, part[:, kt, 1, :], start=False, stop=False)
                    last = mm(out, low, part[:, kt, 0, :], start=False, stop=kt == total - 1)
                return last

            def job_of(off, job, n_out, part, ready=None, total=KT):
                pe.wait_ge(taken, off(1) + (n_out + 1))
                for half in range(2):
                    if ready is not None:
                        pe.wait_ge(*ready(half))
                    count = min(8, total - 8 * half)
                    half_job(off, job, half, bank[job % 4][:, 0:T], part, 8 * half, count,
                             total).then_inc(half_done, 1)

            def v_job(off, job, c, banks, part, ready):
                for half in range(2):
                    pe.wait_ge(low_ready, off(2) + (2 * job + half + 1))
                    for n in range(2):
                        kt = 4 * c + 2 * half + n
                        pe.wait_ge(ready, kt + 1)
                        cols = slice(half * HALF + n * 512, half * HALF + (n + 1) * 512)
                        high, low = w_high[:, job % 2, cols], w_low[:, job % 2, cols]
                        for t in range(QT):
                            tokens = slice(t * P, (t + 1) * P)
                            mm(banks[t][:, :], part[:, kt, 0, tokens], high, start=kt == 0, stop=False)
                            mm(banks[t][:, :], part[:, kt, 0, tokens], low, start=False, stop=False)
                            last = mm(banks[t][:, :], part[:, kt, 1, tokens], high, start=False,
                                      stop=kt == KT - 1)
                    last.then_inc(half_done, 1)

            def norm_sum(norm, out, cols=False):
                pe.wait_ge(acc_made, SUMMED[norm + 1])
                last = mm(out[:, 0:T], ones, acc[:, :], start=True, stop=True)
                for t in range(QT if cols else 0):
                    last = mm(out[:, T + t:T + t + 1], acc[:, t * P:(t + 1) * P], ones[:, 0:1],
                              start=True, stop=True)
                last.then_inc(sum_ready, 1)

            def outputs(out, v, w, first=True, final=True):
                mm(out[:, 0:T], v[:, 0, :], w[:, 0:T], start=first, stop=False)
                return mm(out[:, P:T], v[:, 1, :], w[:, T:CAUSAL], start=False, stop=final)

            def causal_scores(out, q, k):
                mm(out[:, 0:P], q[:, 0:P], k[:, 0:P], start=True, stop=True)
                return mm(out[:, P:CAUSAL], q[:, P:T], k, start=True, stop=True)

            def transposes(out, w):
                for n in range(3):
                    last = nc.tensor.transpose(out[:, n * P:(n + 1) * P], w[:, n * P:(n + 1) * P], ident)
                return last

            with pe.Fori(0, 2) as i:
                for s in range(8):
                    g = s // 4
                    if s % 4 == 0:
                        pe.wait_ge(taken, i * 4 + (2 * g + 2))
                    v_job(by(i, 8), JOB_V + s, s % 4, bank[2 * g:2 * g + 2], part_a, in_low)
            pe.wait_ge(const_landed, 16 * 3)
            norm_sum(N_X, extra[0], True)
            norm_sum(N_MEM, extra[1], True)
            with pe.Fori(0, HEADS_B // 2) as i:
                for s in range(4):
                    job_of(by(i), JOB_B + s, OUT_B + s, part_a)
            with pe.Fori(0, HEADS_C // 2) as i:
                for s in range(4):
                    job_of(by(i), JOB_C + s, OUT_C + s, part_a)
                    if s == 0:
                        pe.wait_ge(held_ready, i * 4 + 4)
                        pe.wait_ge(o_taken, i * 2)
                        for h in range(2):
                            q = qk[:, i * 4 + (SLOT_B + 2 * h), :]
                            mm(extra[h][:, 0:T], held_qk[h][:, 0:P], q, start=True, stop=True)
                            last = mm(extra[h][:, T:CAUSAL], held_qk[h][:, P:T],
                                      qk[:, i * 4 + (SLOT_B + 2 * h), P:T], start=True, stop=True)
                        last.then_inc(s_ready, 1)
                    if s == 1:
                        for h in range(2):
                            pe.wait_ge(soft_ready, i * 2 + (h + 1))
                            mm(extra[2 + h][:, T:CAUSAL], below, soft[h][:, T:CAUSAL], start=True, stop=True)
                            mm(extra[2 + h][:, 0:T], below, soft[h][:, 0:T], start=True, stop=False)
                            last = mm(extra[2 + h][:, P:T], ones, soft[h][:, T:CAUSAL], start=False, stop=True)
                        last.then_inc(t_ready, 1)
                    if s == 2:
                        for h in range(2):
                            pe.wait_ge(w_ready, i * 2 + (h + 1))
                            last = outputs(extra[h], held_v[h], weight[h])
                        last.then_inc(o_ready, 1)
            with pe.Fori(0, HEADS_A // 2) as i:
                for s in range(4):
                    job_of(by(i), JOB_A + s, OUT_A + s, part_a)
                    if s == 0:
                        pe.wait_ge(held_ready, i * 6 + (3 * 4 + 6))
                        pe.wait_ge(o_taken, i + HEADS_B)
                        for g in range(3):
                            k = i * 2 + (SLOT_C + 4 * g + 1)
                            mm(extra[g][:, 0:P], held_qk[g][:, 0:P], qk[:, k, 0:P], start=True, stop=True)
                            last = mm(extra[g][:, P:CAUSAL], held_qk[g][:, P:T], qk[:, k, :],
                                      start=True, stop=True)
                        last.then_inc(s_ready, 1)
                    if s == 1:
                        pe.wait_ge(prob_c, i * 2 + 2)
                        for g in range(3):
                            last = transposes(extra[(g + 3) % 4], scores_c[:, g, :])
                        last.then_inc(t_ready, 1)
                    if s == 2:
                        pe.wait_ge(w_c, i * 3 + 3)
                        for g in range(3):
                            last = outputs(extra[2], held_v[g], weights_c[:, g, :], g == 0, g == 2)
                        last.then_inc(o_ready, 1)
            norm_sum(N_B, extra[3])
            for i in range(HEADS_A // 2):
                for s in range(4):
                    job = JOB_MK + 4 * i + s
                    if i == 0:
                        job_of(none, job, OUT_MK + s, part_b)
                    else:
                        if s == 0:
                            pe.wait_ge(taken, BANKS + OUT_MV - 2)
                        v_job(none, job, s, bank[0:2], part_b, mem_low)
                    if s == 0:
                        pe.wait_ge(o_taken, HEADS_B + MIX_C + 2 * i)
                        for h in range(2):
                            n = 4 * i + 2 * h
                            last = causal_scores(extra[h], qk[:, slot_a(n), :], qk[:, slot_a(n + 1), :])
                        last.then_inc(s_ready, 1)
                    if s == 1:
                        pe.wait_ge(prob_a, 4 * i + 4)
                        pe.wait_ge(log_ready, N_B + 1 + i)
                        for h in range(2):
                            last = transposes(extra[2 + h], score[h])
                        last.then_inc(t_ready, 1)
                    if s == 2:
                        for h in range(2):
                            head = 2 * i + h
                            pe.wait_ge(w_a, 2 * i + h + 1)
                            last = outputs(extra[h], values[:, :, head * P:(head + 1) * P], weight[h])
                        last.then_inc(o_ready, 1)
                if i == 0:
                    norm_sum(N_C, extra[3])
            norm_sum(N_A, extra[3])
            pe.wait_ge(taken, BANKS + OUT_OUT)
            with pe.Fori(0, KT // 4) as i:
                for s in range(4):
                    pe.wait_ge(taken, i * 4 + (OUT_OUT + s + 1))
                    for half in range(2):
                        pe.wait_ge(merged_low, 8 + 4 * half)
                        half_job(by(i), JOB_OUT + s, half, bank[s][:, 0:T], part_a, 8 * half,
                                 8 - 4 * half, MIX).then_inc(half_done, 1)

            def cross_scores(h):
                pe.wait_ge(taken, BANKS + OUT_CQ + h + 1)
                if h >= 2:
                    pe.wait_ge(cross_exp, 2 * h - 2)
                for t in range(QT):
                    last = mm(extra[h % 2][:, t * T:(t + 1) * T], qk[:, SLOT_CQ + h, t * P:(t + 1) * P],
                              qk[:, SLOT_MK + h, :], start=True, stop=True)
                last.then_inc(cross_s, 1)

            def cross_turn(h):
                pe.wait_ge(cross_prob, 2 * h + 2)
                if h >= 2:
                    pe.wait_ge(cross_wt, h - 1)
                for k in range(QT):
                    for t in range(QT):
                        last = nc.tensor.transpose(
                            extra[2 + h % 2][:, k * T + t * P:k * T + (t + 1) * P],
                            cross_p[h % 2][:, t * T + k * P:t * T + (k + 1) * P], ident)
                last.then_inc(cross_t, 1)

            def cross_out(h):
                pe.wait_ge(cross_wt, h + 1)
                for k in range(QT):
                    last = mm(bank[h][:, 0:T], mem_v[:, k, h * P:(h + 1) * P],
                              cross_w[h % 2][:, k * T:(k + 1) * T], start=k == 0, stop=k == QT - 1)
                last.then_inc(cross_o, 1)

            for s in range(4):
                job_of(none, JOB_CQ + s, OUT_OUT + KT + s, part_b,
                       (lambda half: (x1_low, 8 + 8 * half)) if s == 0 else None)
                if s == 0:
                    norm_sum(N_X1, extra[3])
                if s >= 1:
                    cross_scores(s - 1)
                if s >= 2:
                    if s == 2:
                        pe.wait_ge(log_ready, N_X1 + 1)
                    if s == 3:
                        cross_turn(0)
            cross_turn(1)
            cross_out(0)
            cross_scores(3)
            cross_turn(2)
            cross_out(1)
            cross_turn(3)
            cross_out(2)
            cross_out(3)
            pe.wait_ge(taken, BANKS + OUT_CO)
            for s in range(4):
                for half in range(2):
                    for t in (2 * half, 2 * half + 1):
                        pe.wait_ge(taken, OUT_CO + 4 * s + t + 1)
                        last = half_job(none, JOB_CO + s, half, bank[t][:, 0:T], part_b, 0, CROSS, CROSS,
                                        place=4 * (t % 2))
                    last.then_inc(half_done, 1)
            pe.wait_ge(x2_low, KT)
            norm_sum(N_X2, extra[3])

            def mlp_quarter(q):
                with pe.Fori(0, QUARTER // 4) as i:
                    for s in range(4):
                        job_of(lambda k: q * (32 * k) + i * (4 * k), JOB_MLP + s, OUT_MLP + s, part_a)
                with pe.Fori(0, KT // 4) as i:
                    for s in range(4):
                        job_of(lambda k: q * (32 * k) + i * (4 * k), JOB_MLP + QUARTER + s,
                               OUT_MLP + QUARTER + s, part_b,
                               (lambda half: (hid_low, q * 16 + (8 + 8 * half))) if s == 0 else None)

            with pe.Fori(0, 4) as q:
                mlp_quarter(q)
            norm_sum(N_LAST, extra[3])


def shape_constants():
    inverse = (1.0 / (np.float32(THETA) ** (np.arange(0, P, 2, dtype=np.float32) / np.float32(P)))).astype(np.float32)
    angle = (np.arange(T, dtype=np.float32)[:, None] * inverse[None, :]).astype(np.float32).T
    cos, sin = np.cos(angle), np.sin(angle)
    rope = np.stack([np.concatenate([cos, cos]), np.concatenate([-sin, sin])], axis=1)

    query, key = np.arange(T)[:, None], np.arange(T)[None, :]
    def tiles(seen):
        bias = np.where(seen, 0.0, NEG).astype(np.float32)
        return np.concatenate([bias[0:P, 0:P], bias[P:T, :]], axis=1)
    causal = tiles(key <= query)
    past = np.where(key < query, 0.0, NEG).astype(np.float32).T
    past = np.concatenate([past[0:P, :], past[P:T, P:T]], axis=1)
    dilated = [tiles((key <= query) & (query - key <= window) & ((query - key) % step == 0))
               for window, step in PATTERNS]
    masks = np.stack([causal, past] + dilated, axis=1)

    row, col = np.arange(P)[:, None], np.arange(P)[None, :]
    square = np.stack([row == col, row >= 0 * col, row >= col], axis=1)
    return (np.ascontiguousarray(rope, dtype=np.float32), np.ascontiguousarray(masks, dtype=np.float32),
            np.ascontiguousarray(square, dtype=np.float32))


def laid_out(inputs):
    a = {k: np.asarray(v) for k, v in inputs.items()}

    def tokens(v):
        return v.T.reshape(KT, P, T).transpose(1, 0, 2)

    def by_output(w):
        k, n = w.shape[0] // P, w.shape[1] // P
        return w.reshape(k, P, n, P).transpose(2, 1, 0, 3).reshape(n, P, k * P)

    def by_512(w):
        return w.reshape(4, 4, P, -1, 512).transpose(3, 0, 2, 1, 4).reshape(-1, P, CHUNK)

    w_in = a["w_in"][0].reshape(D, 3, HEADS, P)
    order = [*range(HEADS_A, HEADS), *range(HEADS_A)]
    q, k = (w_in[:, n][:, order] for n in range(2))
    wqk = np.stack([q, k], axis=2).reshape(D, 2 * HEADS * P)
    mixed = np.concatenate([a["w_out"][0][HEADS_A * P:], a["w_out"][0][:HEADS_A * P]])
    ckv = a["w_ckv"][0]
    w_co = a["w_co"][0].reshape(CROSS, P, 4, 4, P).transpose(2, 1, 3, 0, 4).reshape(4, P, CHUNK)
    w_down = np.concatenate([by_output(a["w_down"][0][n * D:(n + 1) * D]) for n in range(4)])
    gains = np.concatenate([a["g_mix"][0], a["g_out_b"][0], a["g_out_c"][0], a["g_out_a"][0],
                            a["g_cross"][0], a["g_mem"], a["g_mlp"][0], a["g_final"]]).reshape(GAINS, P).T
    rope, masks, square = shape_constants()
    arrays = {
        "x": tokens(a["x"][0]), "mem": tokens(a["mem"][0]), "wqk": by_output(wqk),
        "wv": by_512(w_in[:, 2].reshape(D, HEADS * P)), "wmk": by_output(ckv[:, :CROSS * P]),
        "wmv": by_512(ckv[:, CROSS * P:]), "wout": by_output(mixed), "wcq": by_output(a["w_cq"][0]),
        "wco": w_co, "wup": by_output(a["w_up"][0]), "wdown": w_down, "gains": gains, "rope": rope,
        "masks": masks, "square": square,
    }
    return {f"in_{name}": np.ascontiguousarray(v) for name, v in arrays.items()}


def kernel(**inputs):
    import concourse.bacc as bacc
    from concourse.bass_utils import run_bass_kernel_spmd

    nc = bacc.Bacc("TRN2", target_bir_lowering=False, num_devices=1)
    arrays = laid_out(inputs)
    args = [nc.dram_tensor(name, a.shape, mybir.dt.from_np(a.dtype), kind="ExternalInput").ap()
            for name, a in arrays.items()]
    args.append(nc.dram_tensor("out", (P, KT, T), mybir.dt.float32, kind="ExternalOutput").ap())
    build(nc, *args)
    result = run_bass_kernel_spmd(nc, [arrays], core_ids=[0]).results[0]["out"]
    return np.ascontiguousarray(result.transpose(2, 1, 0).reshape(1, T, D))
```

```python
from contextlib import ExitStack

import concourse.bass as bass
import numpy as np
from concourse import mybir

D = 2048
T = 256
P = 128
HEADS_A, HEADS_B, HEADS_C = 4, 6, 6
PATTERNS = ((128, 1), (512, 4), (2048, 16))
HEADS = HEADS_A + HEADS_B + HEADS_C
CROSS = 4
D_FF = 4 * D
EPS = 1e-6
SCALE = P ** -0.5
NEG = -1e30
THETA = 10000.0

KT = D // P
QT = T // P
MIX_C = HEADS_C // len(PATTERNS)
MIX = HEADS_A + HEADS_B + MIX_C
QUARTER = D_FF // 4 // P
CHUNK = KT * P
HALF = CHUNK // 2
CAUSAL = P + T

GROUP_V = 4
JOB_V = 0
JOB_B = JOB_V + HEADS * P // 512 * GROUP_V
JOB_C = JOB_B + 2 * HEADS_B
JOB_A = JOB_C + 2 * HEADS_C
JOB_MK = JOB_A + 2 * HEADS_A
JOB_BC = JOB_MK + CROSS
JOB_OA = JOB_BC + KT // 2
JOB_CQ = JOB_OA + KT // 4
JOB_MV = JOB_CQ + CROSS
JOB_CO = JOB_MV + GROUP_V
JOB_MLP = JOB_CO + CROSS
JOBS = JOB_MLP + 4 * 2 * QUARTER

OUT_B = 2 * (HEADS * P // 512)
OUT_C = OUT_B + 2 * HEADS_B
OUT_A = OUT_C + 2 * HEADS_C
OUT_MK = OUT_A + 2 * HEADS_A
OUT_BC = OUT_MK + CROSS
OUT_OA = OUT_BC + KT
OUT_CQ = OUT_OA + KT
OUT_MV = OUT_CQ + CROSS
OUT_CR = OUT_MV + QT
OUT_CO = OUT_CR + CROSS
OUT_MLP = OUT_CO + KT
OUT_PARTS = 4
BANKS = 4

G_MIX, G_OUT, G_CROSS = 0, KT, KT + MIX
G_MEM, G_MLP, G_FINAL = G_CROSS + KT, G_CROSS + 2 * KT, G_CROSS + 3 * KT
GAINS = G_FINAL + KT

SLOT_B, SLOT_C = 0, 4 * HEADS_A
SLOTS = SLOT_C + 2 * HEADS_C
SLOT_MK, SLOT_MV, SLOT_OA, SLOT_CQ = SLOT_C, SLOT_C + CROSS, SLOT_C + 2 * CROSS, 0


def slot_a(n):
    return n * 2 + 1


def slot_o(n):
    return n * 2


def slot_x1(t):
    return t if t < 8 else t + 4 if t < 12 else t - 4


def build(nc, x_in, mem_in, wqk_in, wv_in, wmk_in, wmv_in, wbc_in, woa_in, wcq_in, wco_in,
          wup_in, wdown_in, gains_in, rope_in, masks_in, square_in, out):
    F32, F32R = mybir.dt.float32, mybir.dt.float32r
    ACT, ALU, AX = mybir.ActivationFunctionType, mybir.AluOpType, mybir.AxisListType

    with ExitStack() as ctx:
        def sb(name, shape, dt=F32):
            return ctx.enter_context(nc.sbuf_tensor(name, shape, dt))

        def sem(name):
            return ctx.enter_context(nc.semaphore(name))

        x = sb("x", [P, KT, T])
        part_a = sb("part_a", [P, KT, 2, T], F32R)
        part_b = sb("part_b", [P, KT, 2, T], F32R)
        staged = sb("staged", [P, 4, CHUNK])
        w_high = sb("w_high", [P, 2, CHUNK], F32R)
        w_low = sb("w_low", [P, 2, CHUNK], F32R)
        qk = sb("qk", [P, SLOTS, T])
        values = sb("values", [P, QT, HEADS * P])
        masks = sb("masks", [P, 2 + len(PATTERNS), CAUSAL])
        square = sb("square", [P, 3, P])
        gains = sb("gains", [P, GAINS])
        rope = sb("rope", [P, 2, T])
        spare = sb("spare", [P, 2, T])
        acc = sb("acc", [P, T])
        squares = sb("squares", [P, 2, T])
        factor = sb("factor", [P, 3, T + QT])
        peak, total = sb("peak", [P, 4]), sb("total", [P, 4])
        eps = sb("eps", [P, 1])
        ident, ones, below = square[:, 0, :], square[:, 1, :], square[:, 2, :]
        MASK_A, MASK_B, MASK_C = 0, 1, 2

        flat = x[:, :, :].rearrange("p t n -> p (t n)")
        score = [flat[:, h * CAUSAL:(h + 1) * CAUSAL] for h in range(2)]
        soft = [flat[:, (2 + h) * CAUSAL:(3 + h) * CAUSAL] for h in range(2)]
        weight = [flat[:, (4 + h) * CAUSAL:(5 + h) * CAUSAL] for h in range(2)]
        scores_c = flat[:, 0:3 * CAUSAL].rearrange("p (g n) -> p g n", g=3)
        weights_c = flat[:, 3 * CAUSAL:6 * CAUSAL].rearrange("p (g n) -> p g n", g=3)
        held = 6 * CAUSAL
        held_qk = [flat[:, held + 512 * h:held + 512 * h + T] for h in range(3)]
        held_v = [flat[:, held + 512 * h + T:held + 512 * (h + 1)].rearrange("p (t n) -> p t n", t=QT)
                  for h in range(3)]
        score_a = [values[:, 0, 512 + n * CAUSAL:512 + (n + 1) * CAUSAL] for n in range(2)]
        weight_a = [values[:, 0, 512 + n * CAUSAL:512 + (n + 1) * CAUSAL] for n in range(2, 4)]
        flat_v = values[:, :, :].rearrange("p t n -> p (t n)")
        cross_p = [flat_v[:, h * 512:(h + 1) * 512] for h in range(2)]
        cross_w = [flat_v[:, (2 + h) * 512:(3 + h) * 512] for h in range(4)]
        cross_peak = flat_v[:, 3072:3080]
        cross_bias = flat_v[:, 3080:3088]
        cross_total = flat_v[:, 3088:3096]
        x_gained = values[:, :, :].rearrange("p t n -> p (t n)").rearrange("p (t n) -> p t n", t=KT)
        mem_raw = qk[:, SLOTS - KT:SLOTS, :]
        mem_v = qk[:, SLOT_MV:SLOT_MV + CROSS, :].rearrange("p s n -> p (s n)").rearrange(
            "p (t n) -> p t n", t=QT)

        bank = [ctx.enter_context(nc.psum_tensor(f"bank{n}", [P, 512], F32)) for n in range(BANKS)]
        extra = [ctx.enter_context(nc.psum_tensor(f"extra{n}", [P, 512], F32)) for n in range(4)]

        landed = [sem(f"landed{n}") for n in range(4)]
        high_ready = sem("high_ready")
        low_ready = sem("low_ready")
        half_done = sem("half_done")
        taken = sem("taken")
        first_landed = sem("first_landed")
        wide_moved, wide_added, x_wide = sem("wide_moved"), sem("wide_added"), sem("x_wide")
        x_landed = [sem(f"x_landed{n}") for n in range(4)]
        gains_landed, const_landed, mem_landed, x_again = (
            sem("gains_landed"), sem("const_landed"), sem("mem_landed"), sem("x_again"))
        in_high, in_low, mem_high, mem_low = sem("in_high"), sem("in_low"), sem("mem_high"), sem("mem_low")
        acc_clear, sq_made, acc_made = sem("acc_clear"), sem("sq_made"), sem("acc_made")
        sum_ready, log_ready, factor_ready = sem("sum_ready"), sem("log_ready"), sem("factor_ready")
        rope_ready, v_scaled = sem("rope_ready"), sem("v_scaled")
        turned, rope_made = sem("turned"), sem("rope_made")
        held_ready, s_ready, t_ready, o_ready, o_taken = (
            sem("held_ready"), sem("s_ready"), sem("t_ready"), sem("o_ready"), sem("o_taken"))
        z_ready, abs_ready, exp_ready, ln_ready, soft_ready, logw_ready, w_ready = (
            sem("z_ready"), sem("abs_ready"), sem("exp_ready"), sem("ln_ready"), sem("soft_ready"),
            sem("logw_ready"), sem("w_ready"))
        masked_c, peak_c, exp_c, inv_c, prob_c, w_c = (
            sem(n) for n in ("masked_c", "peak_c", "exp_c", "inv_c", "prob_c", "w_c"))
        masked_a, peak_a, exp_a, inv_a, prob_a, w_a = (
            sem(n) for n in ("masked_a", "peak_a", "exp_a", "inv_a", "prob_a", "w_a"))
        merged, merged_high, merged_low = sem("merged"), sem("merged_high"), sem("merged_low")
        x1_high, x1_low, x2_high, x2_low = sem("x1_high"), sem("x1_low"), sem("x2_high"), sem("x2_low")
        cross_s, cross_max, cross_neg, cross_exp, cross_inv, cross_prob = (
            sem(n) for n in ("cross_s", "cross_max", "cross_neg", "cross_exp", "cross_inv", "cross_prob"))
        cross_t, cross_wt, cross_o, cross_high, cross_low = (
            sem(n) for n in ("cross_t", "cross_wt", "cross_o", "cross_high", "cross_low"))
        up_moved, up_added, act_ready, sq_ready, hid_high, hid_low = (
            sem(n) for n in ("up_moved", "up_added", "act_ready", "sq_ready", "hid_high", "hid_low"))
        x_gain, y_ready, stored = sem("x_gain"), sem("y_ready"), sem("stored")

        block = ctx.enter_context(nc.Block())

        def f32(ap):
            return ap.bitcast(F32)

        def by(i, n=4):
            return lambda k: i * (n * k)

        def none(k):
            return 0

        @block.sync
        def _(sp):
            def load(src, off, job, cols=CHUNK):
                if job >= 4:
                    sp.wait_ge(low_ready, off(2) + (2 * job - 6))
                sp.dma_start(staged[:, job % 4, 0:cols], src).then_inc(landed[job % 4], 16)

            def stream(src, job, count, cols=CHUNK):
                with sp.Fori(0, count // 4) as i:
                    for s in range(4):
                        load(src[i * 4 + s, :, 0:cols], by(i), job + s, cols)

            sp.dma_start(x[:, 0:4, :], x_in[:, 0:4, :]).then_inc(x_landed[0], 16)
            sp.dma_start(staged[:, 0, 0:HALF], wv_in[0, :, 0:HALF]).then_inc(first_landed, 16)
            sp.dma_start(staged[:, 0, HALF:CHUNK], wv_in[0, :, HALF:CHUNK]).then_inc(landed[0], 16)
            for part in range(1, 4):
                sp.dma_start(x[:, 4 * part:4 * part + 4, :],
                             x_in[:, 4 * part:4 * part + 4, :]).then_inc(x_landed[part], 16)
                load(wv_in[part, :, :], none, part)
            with sp.Fori(0, 3) as i:
                for s in range(4):
                    load(wv_in[i * 4 + (4 + s), :, :], by(i), 4 + s)
            stream(wqk_in, JOB_B, 2 * HEADS)
            stream(wmk_in, JOB_MK, CROSS)
            sp.wait_ge(o_ready, 1 + 5)
            sp.dma_start(x[:, :, :], x_in).then_inc(x_again, 16)
            stream(wbc_in, JOB_BC, KT // 2)
            stream(woa_in, JOB_OA, KT // 4)
            stream(wcq_in, JOB_CQ, CROSS)
            stream(wmv_in, JOB_MV, GROUP_V)
            stream(wco_in, JOB_CO, CROSS)
            with sp.Fori(0, 4) as q:
                for part, src in enumerate((wup_in, wdown_in)):
                    with sp.Fori(0, QUARTER // 4) as i:
                        for s in range(4):
                            load(src[q * 16 + i * 4 + s, :, :],
                                 lambda k: q * (32 * k) + i * (4 * k), JOB_MLP + 16 * part + s)
            for part in range(OUT_PARTS):
                tiles = slice(part * KT // OUT_PARTS, (part + 1) * KT // OUT_PARTS)
                sp.wait_ge(y_ready, part + 1)
                sp.dma_start(out[:, tiles, :], x_gained[:, tiles, :]).then_inc(stored, 16)
            sp.wait_ge(stored, 16 * OUT_PARTS)

        SUMMED = [0]
        for tiles in (KT, KT, HEADS_B, MIX_C, HEADS_A, KT, KT, KT):
            SUMMED.append(SUMMED[-1] + tiles)
        N_X, N_MEM, N_B, N_C, N_A, N_X1, N_X2, N_LAST = range(8)
        F_X, F_MEM, F_B, F_C, F_A, F_X1, F_X2, F_LAST = 0, 1, 2, 0, 2, 1, 0, 1

        @block.gpsimd
        def _(pool):
            def clear(norm):
                if norm:
                    pool.wait_ge(sum_ready, norm)
                nc.gpsimd.memset(acc[:, :], 0.0).then_inc(acc_clear, 1)
                pool.wait_ge(acc_clear, norm + 1)

            def add_square(tile, norm, t, off=0):
                n = off + (SUMMED[norm] + t)
                if norm or t:
                    pool.wait_ge(acc_made, n)
                nc.gpsimd.tensor_tensor(squares[:, 0, :], tile, tile, ALU.mult).then_inc(sq_made, 1)
                pool.wait_ge(sq_made, n + 1)
                nc.gpsimd.tensor_tensor(acc[:, :], acc[:, :], squares[:, 0, :], ALU.add).then_inc(acc_made, 1)

            def add_made(norm, t):
                n = SUMMED[norm] + t
                pool.wait_ge(acc_made, n)
                pool.wait_ge(sq_made, n + 1)
                nc.gpsimd.tensor_tensor(acc[:, :], acc[:, :], squares[:, n % 2, :], ALU.add).then_inc(acc_made, 1)

            def merge_low(tile):
                pool.wait_ge(merged_high, tile + 1)
                nc.gpsimd.tensor_tensor(part_a[:, tile, 1, :], spare[:, tile % 2, :],
                                        f32(part_a[:, tile, 0, :]), ALU.subtract).then_inc(merged_low, 1)

            nc.gpsimd.memset(eps[:, :], EPS)
            clear(N_X)
            for t in range(KT):
                if t % 4 == 0:
                    pool.wait_ge(x_landed[t // 4], 16)
                add_square(x[:, t, :], N_X, t)
            clear(N_MEM)
            pool.wait_ge(mem_landed, 16)
            for t in range(KT):
                add_square(mem_raw[:, t, :], N_MEM, t)

            clear(N_B)
            pool.wait_ge(o_taken, 1 + HEADS_B)
            for t in range(HEADS_B):
                add_square(qk[:, slot_o(t), :], N_B, t)
            clear(N_C)
            pool.wait_ge(o_taken, 1 + HEADS_B + MIX_C)
            for t in range(MIX_C):
                add_square(qk[:, slot_o(HEADS_B + t), :], N_C, t)
            for t in range(HEADS_B + MIX_C):
                merge_low(t)
            clear(N_A)
            for t in range(HEADS_A):
                pool.wait_ge(o_taken, 1 + HEADS_B + MIX_C + t + 1)
                add_square(qk[:, SLOT_OA + t, :], N_A, t)
            for t in range(HEADS_B + MIX_C, MIX):
                merge_low(t)
            for norm in (N_X1, N_X2):
                clear(norm)
                for t in range(KT):
                    add_made(norm, t)
            clear(N_LAST)
            with pool.Fori(0, KT // 4) as i:
                for s in range(4):
                    pool.wait_ge(taken, i * 4 + (BANKS + OUT_MLP + 3 * 32 + 16 + s + 1))
                    add_square(x[:, i * 4 + s, :], N_LAST, s, i * 4)

        @block.scalar
        def _(act):
            nc.scalar.preload_act_table_set("natural_log_exp_and_others")
            act.dma_start(gains[:, :], gains_in).then_inc(gains_landed, 16)
            for to, src in ((square, square_in), (rope, rope_in), (masks, masks_in)):
                act.dma_start(to[:, :, :], src).then_inc(const_landed, 16)

            def split(off, job, half):
                if job == 0 and half == 0:
                    act.wait_ge(first_landed, 16)
                elif half == 0 or job == 0:
                    act.wait_ge(landed[job % 4], off(4) + 16 * (job // 4 + 1))
                if job >= 2:
                    act.wait_ge(half_done, off(2) + (2 * (job - 2) + half + 1))
                cols = slice(half * HALF, (half + 1) * HALF)
                nc.scalar.activation(w_high[:, job % 2, cols], staged[:, job % 4, cols],
                                     ACT.Copy).then_inc(high_ready, 1)

            def norm_factor(norm, width, src, slot, cols=T):
                act.wait_ge(sum_ready, norm + 1)
                nc.scalar.activation(factor[:, slot, 0:cols], src[:, 0:cols], ACT.Ln, bias=eps[:, :],
                                     scale=1.0 / width).then_inc(log_ready, 1)
                act.wait_ge(log_ready, norm + 1)
                nc.scalar.activation(factor[:, slot, 0:cols], factor[:, slot, 0:cols], ACT.Exp,
                                     scale=-0.5).then_inc(factor_ready, 1)

            def turn(off, job, n_turn, n_out):
                act.wait_ge(half_done, off(2) + (2 * job + 2))
                act.wait_ge(taken, off(1) + (BANKS + n_out))
                src = bank[job % 4]
                nc.scalar.activation(spare[0:64, 0, :], src[64:P, 0:T], ACT.Copy)
                nc.scalar.activation(spare[64:P, 0, :], src[0:64, 0:T], ACT.Copy).then_inc(turned, 1)

            def move(off, job, n_out, n_wide):
                act.wait_ge(half_done, off(2) + (2 * job + 2))
                act.wait_ge(taken, off(1) + (BANKS + n_out - 1))
                nc.scalar.activation(spare[:, job % 2, :], bank[job % 4][:, T:2 * T],
                                     ACT.Copy).then_inc(wide_moved, 1)

            def mem_part(t):
                nc.scalar.activation(part_b[:, t, 0, :], mem_raw[:, t, :], ACT.Copy,
                                     scale=gains[:, bass.ds(G_MEM + t, 1)]).then_inc(mem_high, 1)

            def query_tile(t):
                return slice(0, P) if t == 0 else slice(P, CAUSAL)

            act.sem_inc(o_taken, 1)
            act.wait_ge(gains_landed, 16)
            for t in range(KT):
                if t % 4 == 0:
                    act.wait_ge(x_landed[t // 4], 16)
                nc.scalar.activation(part_a[:, t, 0, :], x[:, t, :], ACT.Copy,
                                     scale=gains[:, G_MIX + t:G_MIX + t + 1]).then_inc(in_high, 1)
                if t % 4 == 3:
                    for half in range(2):
                        split(none, t // 4, half)
            act.wait_ge(acc_clear, 1)
            for s in range(2, 4):
                for half in range(2):
                    split(none, JOB_V + s + 2, half)
            with act.Fori(1, 3) as i:
                for s in range(4):
                    for half in range(2):
                        split(by(i), JOB_V + s + 2, half)
            act.dma_start(mem_raw, mem_in).then_inc(mem_landed, 16)
            for s in range(4):
                split(none, JOB_V + 12 + s + 2, 0)
                split(none, JOB_V + 12 + s + 2, 1)
                if s == 0:
                    act.wait_ge(mem_landed, 16)
                mem_part(s)
            norm_factor(N_X, D, extra[0], F_X, T + QT)
            act.wait_ge(taken, BANKS + OUT_B)
            act.wait_ge(factor_ready, 1)
            nc.scalar.activation(values[:, 0, :], values[:, 0, :], ACT.Copy,
                                 scale=factor[:, F_X, T:T + 1]).then_inc(v_scaled, 1)
            with act.Fori(0, HEADS_B // 2) as i:
                for s in range(4):
                    split(by(i), JOB_B + s + 2, 0)
                    mem_part(i * 4 + (4 + s))
                    move(by(i), JOB_B + s, OUT_B + s, s)
                    split(by(i), JOB_B + s + 2, 1)
            norm_factor(N_MEM, D, extra[1], F_MEM, T + QT)
            with act.Fori(0, HEADS_C // 2) as i:
                for s in range(4):
                    if s == 3:
                        for h in range(2):
                            act.wait_ge(logw_ready, i * 2 + (h + 1))
                            nc.scalar.activation(weight[h], score[h], ACT.Exp).then_inc(w_ready, 1)
                    split(by(i), JOB_C + s + 2, 0)
                    turn(by(i), JOB_C + s, s, OUT_C + s)
                    if s == 1:
                        for h in range(2):
                            act.wait_ge(abs_ready, i * 2 + (h + 1))
                            nc.scalar.activation(soft[h], soft[h], ACT.Exp, scale=-1.0).then_inc(exp_ready, 1)
                        for h in range(2):
                            act.wait_ge(exp_ready, i * 2 + (h + 1))
                            nc.scalar.activation(soft[h], soft[h], ACT.Ln, bias=1.0).then_inc(ln_ready, 1)
                    split(by(i), JOB_C + s + 2, 1)
                act.wait_ge(o_ready, i + 2)
                for h in range(2):
                    nc.scalar.activation(qk[:, i * 4 + slot_o(h), :], extra[h][:, 0:T],
                                         ACT.Copy).then_inc(o_taken, 1)
            with act.Fori(0, HEADS_A // 2) as i:
                for s in range(4):
                    if s == 3:
                        act.wait_ge(t_ready, i + 4)
                        for g in range(3):
                            nc.scalar.activation(weights_c[:, g, :], extra[(g + 3) % 4][:, 0:CAUSAL],
                                                 ACT.Copy).then_inc(w_c, 1)
                    split(by(i), JOB_A + s + 2, 0)
                    turn(by(i), JOB_A + s, s, OUT_A + s)
                    if s == 1:
                        for t in range(QT):
                            act.wait_ge(peak_c, i * 2 + (t + 1))
                            nc.scalar.activation(scores_c[:, :, query_tile(t)], scores_c[:, :, query_tile(t)],
                                                 ACT.Exp, bias=peak[:, t:t + 1],
                                                 accum_out=total[:, t:t + 1]).then_inc(exp_c, 1)
                    split(by(i), JOB_A + s + 2, 1)
                act.wait_ge(o_ready, i + 5)
                nc.scalar.activation(qk[:, i * 2 + slot_o(HEADS_B), :], extra[2][:, 0:T],
                                     ACT.Copy).then_inc(o_taken, 1)
            norm_factor(N_B, HEADS_B * P, extra[3], F_B)

            def merge_high(tile):
                act.wait_ge(merged, tile + 1)
                nc.scalar.activation(part_a[:, tile, 0, :], spare[:, tile % 2, :],
                                     ACT.Copy).then_inc(merged_high, 1)

            def group_a(i, s):
                if s == 1:
                    for n in range(4):
                        at = score_a[n // 2][:, query_tile(n % 2)]
                        act.wait_ge(peak_a, 4 * i + n + 1)
                        nc.scalar.activation(at, at, ACT.Exp, bias=peak[:, n:n + 1],
                                             accum_out=total[:, n:n + 1]).then_inc(exp_a, 1)
                if s == 2:
                    act.wait_ge(inv_a, i + 1)
                    for n in range(4):
                        at = score_a[n // 2][:, query_tile(n % 2)]
                        nc.scalar.activation(at, at, ACT.Copy, scale=total[:, n:n + 1]).then_inc(prob_a, 1)
                if s == 3:
                    act.wait_ge(t_ready, 6 + i)
                    for h in range(2):
                        nc.scalar.activation(weight_a[h], extra[2 + h][:, 0:CAUSAL], ACT.Copy).then_inc(w_a, 1)

            def outputs_a(i):
                act.wait_ge(o_ready, 1 + 6 + i)
                for h in range(2):
                    nc.scalar.activation(qk[:, SLOT_OA + 2 * i + h, :], extra[h][:, 0:T],
                                         ACT.Copy).then_inc(o_taken, 1)

            for s in range(4):
                group_a(0, s)
                split(none, JOB_MK + s + 2, 0)
                if s == 2:
                    norm_factor(N_C, MIX_C * P, extra[3], F_C)
                merge_high(2 * s)
                merge_high(2 * s + 1)
                split(none, JOB_MK + s + 2, 1)
            outputs_a(0)
            for s in range(8):
                if s < 4:
                    group_a(1, s)
                split(none, JOB_BC + s + 2, 0)
                if s == 6:
                    norm_factor(N_A, HEADS_A * P, extra[3], F_A)
                if s >= 6:
                    merge_high(2 * s - 4)
                    merge_high(2 * s - 3)
                split(none, JOB_BC + s + 2, 1)
                if s == 3:
                    outputs_a(1)

            def grow(job, n_out, norm, part, slot, gain, ready, free):
                for s in range(4):
                    for half in range(2):
                        split(none, job + s + 2, half)
                        tiles = (4 * s + 2 * half, 4 * s + 2 * half + 1)
                        for t in tiles:
                            act.wait_ge(taken, BANKS + n_out + t + 1)
                            if t == 12:
                                act.wait_ge(half_done, free)
                            nc.scalar.activation(part[:, slot(t), 0, :], x[:, t, :], ACT.Copy,
                                                 scale=gains[:, gain + t:gain + t + 1]).then_inc(ready, 1)
                        for t in tiles:
                            n = SUMMED[norm] + t
                            act.wait_ge(acc_made, n - 1)
                            nc.scalar.activation(squares[:, n % 2, :], x[:, t, :], ACT.Square).then_inc(sq_made, 1)

            grow(JOB_OA, OUT_OA, N_X1, part_a, slot_x1, G_CROSS, x1_high, 2 * JOB_CQ)

            def cross_exps(h):
                if h >= 2:
                    act.wait_ge(cross_t, h - 1)
                for t in range(QT):
                    n = 2 * h + t
                    act.wait_ge(cross_neg, n + 1)
                    nc.scalar.activation(cross_p[h % 2][:, t * T:(t + 1) * T], extra[h % 2][:, t * T:(t + 1) * T],
                                         ACT.Exp, bias=cross_bias[:, n:n + 1], scale=SCALE,
                                         accum_out=cross_total[:, n:n + 1]).then_inc(cross_exp, 1)

            def cross_weights(h):
                act.wait_ge(cross_t, h + 1)
                nc.scalar.activation(cross_w[h], extra[2 + h % 2][:, :], ACT.Copy).then_inc(cross_wt, 1)

            for s in range(8):
                split(none, JOB_CQ + s + 2, 0)
                if s < 4:
                    if s == 0:
                        norm_factor(N_X1, D, extra[3], F_X1)
                    move(none, JOB_CQ + s, OUT_CQ + s, s)
                if 2 <= s < 6:
                    cross_exps(s - 2)
                if s >= 4:
                    cross_weights(s - 4)
                split(none, JOB_CQ + s + 2, 1)
            for h in range(CROSS):
                act.wait_ge(cross_o, h + 1)
                nc.scalar.activation(part_b[:, h, 0, :], bank[(h + 2) % 4][:, 0:T], ACT.Copy).then_inc(cross_high, 1)
            grow(JOB_CO, OUT_CO, N_X2, part_a, lambda t: t, G_MLP, x2_high, 1)
            norm_factor(N_X2, D, extra[3], F_X2)

            def mlp_quarter(q, last):
                with act.Fori(0, QUARTER // 4) as i:
                    for s in range(4):
                        n = q * 16 + i * 4 + s
                        off = lambda k: q * (32 * k) + i * (4 * k)
                        split(off, JOB_MLP + s + 2, 0)
                        act.wait_ge(half_done, off(2) + (2 * (JOB_MLP + s) + 2))
                        act.wait_ge(hid_low, n + 1)
                        nc.scalar.activation(spare[:, 1, :], bank[s][:, T:2 * T], ACT.Copy).then_inc(up_moved, 1)
                        act.wait_ge(act_ready, n + 1)
                        nc.scalar.activation(spare[:, 1, :], spare[:, 0, :], ACT.Square).then_inc(sq_ready, 1)
                        act.wait_ge(sq_ready, n + 1)
                        nc.scalar.activation(part_b[:, i * 4 + s, 0, :], spare[:, 1, :], ACT.Copy).then_inc(hid_high, 1)
                        split(lambda k: q * (32 * k) + i * (4 * k), JOB_MLP + s + 2, 1)
                def gained(i, s):
                    act.wait_ge(taken, i * 4 + (BANKS + OUT_MLP + 3 * 32 + 16 + s + 1))
                    nc.scalar.activation(x_gained[:, i * 4 + s, :], x[:, i * 4 + s, :], ACT.Copy,
                                         scale=gains[:, bass.ds(i * 4 + (G_FINAL + s), 1)]).then_inc(x_gain, 1)

                with act.Fori(0, KT // 4 - last) as i:
                    for s in range(4):
                        for half in range(2):
                            split(lambda k: q * (32 * k) + i * (4 * k), JOB_MLP + QUARTER + s + 2, half)
                        if last:
                            gained(i, s)
                if last:
                    for s in range(4):
                        for half in range(2 if s < 2 else 0):
                            split(none, JOBS - 4 + s + 2, half)
                        gained(3, s)

            with act.Fori(0, 3) as q:
                mlp_quarter(q, 0)
            mlp_quarter(3, 1)
            norm_factor(N_LAST, D, extra[3], F_LAST)

        @block.vector
        def _(dve):
            tt = nc.vector.tensor_tensor
            stt = nc.vector.scalar_tensor_tensor

            def split(off, job, half):
                dve.wait_ge(high_ready, off(2) + (2 * job + half + 1))
                cols = slice(half * HALF, (half + 1) * HALF)
                tt(w_low[:, job % 2, cols], staged[:, job % 4, cols], f32(w_high[:, job % 2, cols]),
                   ALU.subtract).then_inc(low_ready, 1)

            def done(off, job):
                dve.wait_ge(half_done, off(2) + (2 * job + 2))

            def roped(off, slot, n_turn, n_out, job):
                done(off, job)
                src = bank[job % 4]
                dve.wait_ge(turned, off(1) + (n_turn + 1))
                tt(spare[:, 1, :], src[:, 0:T], rope[:, 0, :], ALU.mult).then_inc(rope_made, 1)
                tt(spare[:, 0, :], spare[:, 0, :], rope[:, 1, :], ALU.mult).then_inc(rope_made, 1)
                dve.wait_ge(rope_made, off(2) + (2 * n_turn + 2))
                tt(slot, spare[:, 0, :], spare[:, 1, :], ALU.add).then_inc(taken, 1)

            def added(off, job, n_wide, dst, fac):
                dve.wait_ge(wide_moved, off(1) + (n_wide + 1))
                at = spare[:, job % 2, :]
                tt(at, at, bank[job % 4][:, 0:T], ALU.add).then_inc(wide_added, 1)
                dve.wait_ge(wide_added, off(1) + (n_wide + 1))
                tt(dst, at, fac, ALU.mult).then_inc(taken, 1)

            def mem_part(t):
                dve.wait_ge(mem_high, t + 1)
                stt(part_b[:, t, 1, :], mem_raw[:, t, :], gains[:, bass.ds(G_MEM + t, 1)],
                    f32(part_b[:, t, 0, :]), ALU.mult, ALU.subtract).then_inc(mem_low, 1)

            def query_tile(t):
                return slice(0, P) if t == 0 else slice(P, CAUSAL)

            def hold(it, pairs):
                dve.wait_ge(o_ready, it + 1)
                for to, at in pairs:
                    nc.vector.tensor_copy(to, at).then_inc(held_ready, 1)

            dve.sem_inc(taken, BANKS)
            dve.sem_inc(hid_low, 1)
            for t in range(KT):
                dve.wait_ge(in_high, t + 1)
                stt(part_a[:, t, 1, :], x[:, t, :], gains[:, G_MIX + t:G_MIX + t + 1],
                    f32(part_a[:, t, 0, :]), ALU.mult, ALU.subtract).then_inc(in_low, 1)
                if t % 4 == 3:
                    for half in range(2):
                        split(none, t // 4, half)
            for g in range(4):
                for s in range(4):
                    job = JOB_V + 4 * g + s
                    if job < 2:
                        continue
                    split(none, job + 2, 0)
                    if s == 3:
                        done(none, job)
                        for t in range(QT):
                            nc.vector.tensor_copy(values[:, t, g * 512:(g + 1) * 512],
                                                  bank[g % 2 * 2 + t][:, :]).then_inc(taken, 1)
                    split(none, job + 2, 1)
                    if g == 3:
                        mem_part(s)
            dve.wait_ge(const_landed, 16 * 3)
            dve.wait_ge(factor_ready, 1)
            dve.wait_ge(taken, BANKS + OUT_B)
            nc.vector.tensor_scalar(values[:, 1, :], values[:, 1, :], factor[:, F_X, T + 1:T + 2], None,
                                    ALU.mult).then_inc(v_scaled, 1)
            for n in range(2):
                tt(rope[:, n, :], rope[:, n, :], factor[:, F_X, 0:T], ALU.mult).then_inc(rope_ready, 1)
            with dve.Fori(0, HEADS_B // 2) as i:
                for s in range(4):
                    split(by(i), JOB_B + s + 2, 0)
                    mem_part(i * 4 + (4 + s))
                    added(by(i), JOB_B + s, s, qk[:, i * 4 + (SLOT_B + s), :], factor[:, F_X, 0:T])
                    split(by(i), JOB_B + s + 2, 1)
            dve.wait_ge(rope_ready, 2)
            dve.wait_ge(mem_low, KT)
            dve.wait_ge(factor_ready, 2)
            dve.wait_ge(v_scaled, 2)
            dve.wait_ge(taken, BANKS + OUT_C)
            with dve.Fori(0, HEADS_C // 2) as i:
                hold(i, [(held_qk[h], qk[:, i * 4 + (SLOT_B + 2 * h + 1), :]) for h in range(2)]
                     + [(held_v[h], values[:, :, bass.ds(i * 256 + (HEADS_A + h) * P, P)])
                        for h in range(2)])
                for s in range(4):
                    split(by(i), JOB_C + s + 2, 0)
                    roped(by(i), qk[:, i * 4 + (SLOT_C + s), :], s, OUT_C + s, JOB_C + s)
                    split(by(i), JOB_C + s + 2, 1)
                    if s == 0:
                        dve.wait_ge(s_ready, i + 1)
                        for h in range(2):
                            stt(score[h], extra[h][:, 0:CAUSAL], SCALE, masks[:, MASK_B, :],
                                ALU.mult, ALU.add).then_inc(z_ready, 1)
                        for h in range(2):
                            dve.wait_ge(z_ready, i * 2 + (h + 1))
                            stt(soft[h], score[h], -1.0, score[h], ALU.mult, ALU.max).then_inc(abs_ready, 1)
                    if s == 1:
                        for h in range(2):
                            dve.wait_ge(ln_ready, i * 2 + (h + 1))
                            stt(soft[h], score[h], 0.0, soft[h], ALU.max, ALU.add).then_inc(soft_ready, 1)
                    if s == 2:
                        dve.wait_ge(t_ready, i + 1)
                        for h in range(2):
                            tt(score[h], score[h], extra[2 + h][:, 0:CAUSAL], ALU.subtract).then_inc(logw_ready, 1)
            dve.wait_ge(taken, BANKS + OUT_A)
            with dve.Fori(0, HEADS_A // 2) as i:
                hold(i + 3, [(held_qk[g], qk[:, i * 2 + (SLOT_C + 4 * g), :]) for g in range(3)]
                     + [(held_v[g], values[:, :, bass.ds(i * P + (HEADS_A + HEADS_B + 2 * g) * P, P)])
                        for g in range(3)])
                for s in range(4):
                    split(by(i), JOB_A + s + 2, 0)
                    roped(by(i), qk[:, i * 8 + slot_a(s), :], 2 * HEADS_C + s, OUT_A + s, JOB_A + s)
                    split(by(i), JOB_A + s + 2, 1)
                    if s == 0:
                        dve.wait_ge(s_ready, i + 4)
                        for g in range(3):
                            stt(scores_c[:, g, :], extra[g][:, 0:CAUSAL], SCALE, masks[:, MASK_C + g, :],
                                ALU.mult, ALU.add).then_inc(masked_c, 1)
                        dve.wait_ge(masked_c, i * 3 + 3)
                        for t in range(QT):
                            nc.vector.tensor_reduce(peak[:, t:t + 1], scores_c[:, :, query_tile(t)], AX.XY,
                                                    ALU.max, negate=True).then_inc(peak_c, 1)
                    if s == 1:
                        dve.wait_ge(exp_c, i * 2 + 2)
                        nc.vector.reciprocal(total[:, 0:2], total[:, 0:2]).then_inc(inv_c, 1)
                        dve.wait_ge(inv_c, i + 1)
                        for t in range(QT):
                            nc.vector.tensor_scalar(scores_c[:, :, query_tile(t)], scores_c[:, :, query_tile(t)],
                                                    total[:, t:t + 1], None, ALU.mult).then_inc(prob_c, 1)

            def merge(tile):
                src = (qk[:, slot_o(tile), :] if tile < HEADS_B + MIX_C
                       else qk[:, SLOT_OA + tile - HEADS_B - MIX_C, :])
                norm, slot = ((N_B, F_B) if tile < HEADS_B else (N_C, F_C) if tile < HEADS_B + MIX_C
                              else (N_A, F_A))
                dve.wait_ge(factor_ready, norm + 1)
                if tile >= 2:
                    dve.wait_ge(merged_low, tile - 1)
                stt(spare[:, tile % 2, :], src, gains[:, G_OUT + tile:G_OUT + tile + 1],
                    factor[:, slot, 0:T], ALU.mult, ALU.mult).then_inc(merged, 1)

            def group_a(i, s):
                if s == 0:
                    dve.wait_ge(s_ready, 6 + i)
                    for h in range(2):
                        stt(score_a[h], extra[h][:, 0:CAUSAL], SCALE, masks[:, MASK_A, :],
                            ALU.mult, ALU.add).then_inc(masked_a, 1)
                    for n in range(4):
                        dve.wait_ge(masked_a, 2 * i + n // 2 + 1)
                        nc.vector.tensor_reduce(peak[:, n:n + 1], score_a[n // 2][:, query_tile(n % 2)],
                                                AX.X, ALU.max, negate=True).then_inc(peak_a, 1)
                if s == 1:
                    dve.wait_ge(exp_a, 4 * i + 4)
                    nc.vector.reciprocal(total[:, 0:4], total[:, 0:4]).then_inc(inv_a, 1)

            dve.wait_ge(taken, BANKS + OUT_MK)
            for s in range(4):
                job = JOB_MK + s
                merge(2 * s)
                merge(2 * s + 1)
                split(none, job + 2, 0)
                done(none, job)
                tt(qk[:, SLOT_MK + s, :], bank[s][:, 0:T], factor[:, F_MEM, 0:T], ALU.mult).then_inc(taken, 1)
                split(none, job + 2, 1)
                group_a(0, s)
            dve.wait_ge(x_again, 16)
            for s in range(8):
                job = JOB_BC + s
                if s >= 6:
                    merge(2 * s - 4)
                    merge(2 * s - 3)
                for half in range(2):
                    t = 2 * s + half
                    split(none, job + 2, half)
                    dve.wait_ge(half_done, 2 * job + half + 1)
                    tt(x[:, t, :], x[:, t, :], bank[t % 4][:, 0:T], ALU.add).then_inc(x_wide, 1)
                    dve.wait_ge(x_wide, t + 1)
                    tt(x[:, t, :], x[:, t, :], bank[t % 4][:, T:2 * T], ALU.add).then_inc(taken, 1)
                if s < 4:
                    group_a(1, s)

            def grow(job, n_out, part, slot, gain, high, low):
                def lows(tiles):
                    for t in tiles:
                        dve.wait_ge(high, t + 1)
                        stt(part[:, slot(t), 1, :], x[:, t, :], gains[:, gain + t:gain + t + 1],
                            f32(part[:, slot(t), 0, :]), ALU.mult, ALU.subtract).then_inc(low, 1)

                for s in range(4):
                    for half in range(2):
                        t = 4 * s + 2 * half
                        dve.wait_ge(half_done, 2 * (job + s) + half + 1)
                        for n in (t, t + 1):
                            tt(x[:, n, :], x[:, n, :], bank[n % 4][:, 0:T], ALU.add).then_inc(taken, 1)
                        if t:
                            lows((t - 2, t - 1))
                        split(none, job + s + 2, half)
                lows((KT - 2, KT - 1))

            dve.wait_ge(taken, BANKS + OUT_OA)
            grow(JOB_OA, OUT_OA, part_a, slot_x1, G_CROSS, x1_high, x1_low)

            def cross_peaks(h):
                dve.wait_ge(cross_s, h + 1)
                nc.vector.tensor_reduce(cross_peak[:, 2 * h:2 * h + 2],
                                        extra[h % 2][:, :].rearrange("p (t n) -> p t n", t=QT), AX.X,
                                        ALU.max).then_inc(cross_max, 1)
                dve.wait_ge(cross_max, h + 1)
                nc.vector.tensor_scalar(cross_bias[:, 2 * h:2 * h + 2], cross_peak[:, 2 * h:2 * h + 2],
                                        -SCALE, None, ALU.mult).then_inc(cross_neg, 2)

            def cross_probs(h):
                dve.wait_ge(cross_exp, 2 * h + 2)
                nc.vector.reciprocal(cross_total[:, 2 * h:2 * h + 2],
                                     cross_total[:, 2 * h:2 * h + 2]).then_inc(cross_inv, 1)
                dve.wait_ge(cross_inv, h + 1)
                for t in range(QT):
                    cols = slice(t * T, (t + 1) * T)
                    nc.vector.tensor_scalar(cross_p[h % 2][:, cols], cross_p[h % 2][:, cols],
                                            cross_total[:, 2 * h + t:2 * h + t + 1], None,
                                            ALU.mult).then_inc(cross_prob, 1)

            for s in range(8):
                split(none, JOB_CQ + s + 2, 0)
                if s == 0:
                    dve.wait_ge(factor_ready, N_X1 + 1)
                if s < 4:
                    added(none, JOB_CQ + s, 2 * HEADS_B + s, qk[:, SLOT_CQ + s, :], factor[:, F_X1, 0:T])
                if s == 7:
                    done(none, JOB_CQ + s)
                    for t in range(QT):
                        nc.vector.tensor_scalar(mem_v[:, t, :], bank[t][:, :],
                                                factor[:, F_MEM, T + t:T + t + 1], None,
                                                ALU.mult).then_inc(taken, 1)
                split(none, JOB_CQ + s + 2, 1)
                if 1 <= s < 5:
                    cross_peaks(s - 1)
                if 2 <= s < 6:
                    cross_probs(s - 2)
            for h in range(CROSS):
                dve.wait_ge(cross_high, h + 1)
                tt(part_b[:, h, 1, :], bank[(h + 2) % 4][:, 0:T], f32(part_b[:, h, 0, :]),
                   ALU.subtract).then_inc(taken, 1)
            grow(JOB_CO, OUT_CO, part_a, lambda t: t, G_MLP, x2_high, x2_low)

            def mlp_quarter(q, last):
                with dve.Fori(0, QUARTER // 4) as i:
                    for s in range(4):
                        n = q * 16 + i * 4 + s
                        off = lambda k: q * (32 * k) + i * (4 * k)
                        split(off, JOB_MLP + s + 2, 0)
                        dve.wait_ge(up_moved, n + 1)
                        tt(spare[:, 0, :], spare[:, 1, :], bank[s][:, 0:T], ALU.add).then_inc(up_added, 1)
                        dve.wait_ge(up_added, n + 1)
                        stt(spare[:, 0, :], spare[:, 0, :], 0.0, factor[:, F_X2, 0:T],
                            ALU.max, ALU.mult).then_inc(act_ready, 1)
                        dve.sem_inc(taken, 1)
                        dve.wait_ge(hid_high, n + 1)
                        tt(part_b[:, i * 4 + s, 1, :], spare[:, 1, :], f32(part_b[:, i * 4 + s, 0, :]),
                           ALU.subtract).then_inc(hid_low, 1)
                        split(off, JOB_MLP + s + 2, 1)

                def down(i, s):
                    n = q * 16 + i * 4 + (KT + s + 1)
                    off = lambda k: q * (32 * k) + i * (4 * k)
                    done(off, JOB_MLP + QUARTER + s)
                    tt(x[:, i * 4 + s, :], x[:, i * 4 + s, :], bank[s][:, 0:T], ALU.add).then_inc(x_wide, 1)
                    dve.wait_ge(x_wide, n)
                    tt(x[:, i * 4 + s, :], x[:, i * 4 + s, :], bank[s][:, T:2 * T], ALU.add).then_inc(taken, 1)

                with dve.Fori(0, KT // 4 - last) as i:
                    for s in range(4):
                        off = lambda k: q * (32 * k) + i * (4 * k)
                        split(off, JOB_MLP + QUARTER + s + 2, 0)
                        down(i, s)
                        split(off, JOB_MLP + QUARTER + s + 2, 1)
                if last:
                    for s in range(4):
                        if s < 2:
                            split(none, JOBS - 4 + s + 2, 0)
                        down(3, s)
                        if s < 2:
                            split(none, JOBS - 4 + s + 2, 1)

            dve.wait_ge(factor_ready, N_X2 + 1)
            dve.wait_ge(taken, BANKS + OUT_MLP)
            with dve.Fori(0, 3) as q:
                mlp_quarter(q, 0)
            mlp_quarter(3, 1)
            dve.wait_ge(factor_ready, N_LAST + 1)
            dve.wait_ge(x_gain, KT)
            for part in range(OUT_PARTS):
                tiles = slice(part * KT // OUT_PARTS, (part + 1) * KT // OUT_PARTS)
                tt(x_gained[:, tiles, :], x_gained[:, tiles, :],
                   factor[:, F_LAST:F_LAST + 1, 0:T].to_broadcast([P, KT // OUT_PARTS, T]),
                   ALU.mult).then_inc(y_ready, 1)

        @block.tensor
        def _(pe):
            mm = nc.tensor.matmul

            def half_job(off, job, half, out, part, tiles, count=8, total=KT, place=0, wide=True,
                         slot=lambda kt: kt, waits={}):
                pe.wait_ge(low_ready, off(2) + (2 * job + half + 1))
                for n in range(count):
                    if n in waits:
                        pe.wait_ge(hid_low, waits[n])
                    kt = tiles + n
                    cols = slice(half * HALF + (place + n) * P, half * HALF + (place + n + 1) * P)
                    high, low = w_high[:, job % 2, cols], w_low[:, job % 2, cols]
                    first, last_tile = kt == 0, kt == total - 1
                    if wide:
                        both = part[:, slot(kt), :, :].rearrange("p a n -> p (a n)")
                        if first:
                            mm(out[:, :], high, both, start=True, stop=False)
                        last = mm(out[:, 0:T], low, part[:, slot(kt), 0, :], start=False, stop=False)
                        if not first:
                            last = mm(out[:, :], high, both, start=False, stop=last_tile)
                    else:
                        mm(out[:, 0:T], high, part[:, slot(kt), 0, :], start=first, stop=False)
                        mm(out[:, 0:T], high, part[:, slot(kt), 1, :], start=False, stop=False)
                        last = mm(out[:, 0:T], low, part[:, slot(kt), 0, :], start=False, stop=last_tile)
                return last

            def job_of(off, job, n_out, part, ready=None, wide=True, slot=lambda kt: kt):
                pe.wait_ge(taken, off(1) + (n_out + 1))
                for half in range(2):
                    if ready is not None:
                        pe.wait_ge(*ready(half))
                    half_job(off, job, half, bank[job % 4], part, 8 * half, wide=wide,
                             slot=slot).then_inc(half_done, 1)

            def short_jobs(job, n_out, part, at):
                for s in range(4):
                    for half in range(2):
                        for t in (2 * half, 2 * half + 1):
                            pe.wait_ge(taken, n_out + 4 * s + t + 1)
                            last = half_job(none, job + s, half, bank[t], part, 0, 4, 4,
                                            place=4 * (t % 2), wide=False, slot=lambda kt: at + kt)
                        last.then_inc(half_done, 1)

            def v_job(off, job, c, banks, part, ready):
                for half in range(2):
                    pe.wait_ge(low_ready, off(2) + (2 * job + half + 1))
                    for n in range(2):
                        kt = 4 * c + 2 * half + n
                        pe.wait_ge(ready, kt + 1)
                        cols = slice(half * HALF + n * 512, half * HALF + (n + 1) * 512)
                        high, low = w_high[:, job % 2, cols], w_low[:, job % 2, cols]
                        for t in range(QT):
                            tokens = slice(t * P, (t + 1) * P)
                            mm(banks[t][:, :], part[:, kt, 0, tokens], high, start=kt == 0, stop=False)
                            mm(banks[t][:, :], part[:, kt, 0, tokens], low, start=False, stop=False)
                            last = mm(banks[t][:, :], part[:, kt, 1, tokens], high, start=False,
                                      stop=kt == KT - 1)
                    last.then_inc(half_done, 1)

            def norm_sum(norm, out, cols=False):
                pe.wait_ge(acc_made, SUMMED[norm + 1])
                last = mm(out[:, 0:T], ones, acc[:, :], start=True, stop=True)
                for t in range(QT if cols else 0):
                    last = mm(out[:, T + t:T + t + 1], acc[:, t * P:(t + 1) * P], ones[:, 0:1],
                              start=True, stop=True)
                last.then_inc(sum_ready, 1)

            def outputs(out, v, w, first=True, final=True):
                mm(out[:, 0:T], v[:, 0, :], w[:, 0:T], start=first, stop=False)
                return mm(out[:, P:T], v[:, 1, :], w[:, T:CAUSAL], start=False, stop=final)

            def causal_scores(out, q, k):
                mm(out[:, 0:P], q[:, 0:P], k[:, 0:P], start=True, stop=True)
                return mm(out[:, P:CAUSAL], q[:, P:T], k, start=True, stop=True)

            def transposes(out, w):
                for n in range(3):
                    last = nc.tensor.transpose(out[:, n * P:(n + 1) * P], w[:, n * P:(n + 1) * P], ident)
                return last

            pe.sem_inc(o_ready, 1)
            with pe.Fori(0, 2) as i:
                for s in range(8):
                    g = s // 4
                    if s % 4 == 0:
                        pe.wait_ge(taken, i * 4 + (2 * g + 2))
                    v_job(by(i, 8), JOB_V + s, s % 4, bank[2 * g:2 * g + 2], part_a, in_low)
            pe.wait_ge(const_landed, 16 * 3)
            norm_sum(N_X, extra[0], True)
            with pe.Fori(0, HEADS_B // 2) as i:
                for s in range(4):
                    job_of(by(i), JOB_B + s, OUT_B + s, part_a)
            norm_sum(N_MEM, extra[1], True)
            with pe.Fori(0, HEADS_C // 2) as i:
                for s in range(4):
                    job_of(by(i), JOB_C + s, OUT_C + s, part_a, wide=False)
                    if s == 0:
                        pe.wait_ge(held_ready, i * 4 + 4)
                        pe.wait_ge(log_ready, 2)
                        pe.wait_ge(o_taken, i * 2 + 1)
                        for h in range(2):
                            q = qk[:, i * 4 + (SLOT_B + 2 * h), :]
                            mm(extra[h][:, 0:T], held_qk[h][:, 0:P], q, start=True, stop=True)
                            last = mm(extra[h][:, T:CAUSAL], held_qk[h][:, P:T],
                                      qk[:, i * 4 + (SLOT_B + 2 * h), P:T], start=True, stop=True)
                        last.then_inc(s_ready, 1)
                    if s == 2:
                        for h in range(2):
                            pe.wait_ge(soft_ready, i * 2 + (h + 1))
                            mm(extra[2 + h][:, T:CAUSAL], below, soft[h][:, T:CAUSAL], start=True, stop=True)
                            mm(extra[2 + h][:, 0:T], below, soft[h][:, 0:T], start=True, stop=False)
                            last = mm(extra[2 + h][:, P:T], ones, soft[h][:, T:CAUSAL], start=False, stop=True)
                        last.then_inc(t_ready, 1)
                    if s == 3:
                        for h in range(2):
                            pe.wait_ge(w_ready, i * 2 + (h + 1))
                            last = outputs(extra[h], held_v[h], weight[h])
                        last.then_inc(o_ready, 1)
            with pe.Fori(0, HEADS_A // 2) as i:
                for s in range(4):
                    job_of(by(i), JOB_A + s, OUT_A + s, part_a, wide=False)
                    if s == 0:
                        pe.wait_ge(held_ready, i * 6 + (3 * 4 + 6))
                        pe.wait_ge(o_taken, i + (1 + HEADS_B))
                        for g in range(3):
                            k = i * 2 + (SLOT_C + 4 * g + 1)
                            mm(extra[g][:, 0:P], held_qk[g][:, 0:P], qk[:, k, 0:P], start=True, stop=True)
                            last = mm(extra[g][:, P:CAUSAL], held_qk[g][:, P:T], qk[:, k, :],
                                      start=True, stop=True)
                        last.then_inc(s_ready, 1)
                    if s == 2:
                        pe.wait_ge(prob_c, i * 2 + 2)
                        for g in range(3):
                            last = transposes(extra[(g + 3) % 4], scores_c[:, g, :])
                        last.then_inc(t_ready, 1)
                    if s == 3:
                        pe.wait_ge(w_c, i * 3 + 3)
                        for g in range(3):
                            last = outputs(extra[2], held_v[g], weights_c[:, g, :], g == 0, g == 2)
                        last.then_inc(o_ready, 1)
            norm_sum(N_B, extra[3])

            def group_a(i, s):
                if s == 0:
                    pe.wait_ge(o_taken, 1 + HEADS_B + MIX_C + 2 * i)
                    for h in range(2):
                        n = 4 * i + 2 * h
                        last = causal_scores(extra[h], qk[:, slot_a(n), :], qk[:, slot_a(n + 1), :])
                    last.then_inc(s_ready, 1)
                if s == 2:
                    pe.wait_ge(prob_a, 4 * i + 4)
                    pe.wait_ge(log_ready, N_C + 1)
                    for h in range(2):
                        last = transposes(extra[2 + h], score_a[h])
                    last.then_inc(t_ready, 1)
                if s == 3:
                    for h in range(2):
                        head = 2 * i + h
                        pe.wait_ge(w_a, 2 * i + h + 1)
                        last = outputs(extra[h], values[:, :, head * P:(head + 1) * P], weight_a[h])
                    last.then_inc(o_ready, 1)

            for s in range(4):
                job_of(none, JOB_MK + s, OUT_MK + s, part_b, wide=False)
                group_a(0, s)
                if s == 1:
                    pe.wait_ge(log_ready, N_B + 1)
                    norm_sum(N_C, extra[3])
            for s in range(8):
                for half in range(2):
                    t = 2 * s + half
                    pe.wait_ge(taken, OUT_BC + t + 1)
                    pe.wait_ge(merged_low, 8)
                    half_job(none, JOB_BC + s, half, bank[t % 4], part_a, 0, 8, 8).then_inc(half_done, 1)
                if s < 4:
                    group_a(1, s)
                if s == 5:
                    norm_sum(N_A, extra[3])
            pe.wait_ge(merged_low, MIX)
            short_jobs(JOB_OA, OUT_OA, part_a, HEADS_B + MIX_C)

            def cross_scores(h):
                pe.wait_ge(taken, BANKS + OUT_CQ + h + 1)
                if h >= 2:
                    pe.wait_ge(cross_exp, 2 * h - 2)
                for t in range(QT):
                    last = mm(extra[h % 2][:, t * T:(t + 1) * T], qk[:, SLOT_CQ + h, t * P:(t + 1) * P],
                              qk[:, SLOT_MK + h, :], start=True, stop=True)
                last.then_inc(cross_s, 1)

            def cross_turn(h):
                pe.wait_ge(cross_prob, 2 * h + 2)
                if h >= 2:
                    pe.wait_ge(cross_wt, h - 1)
                for k in range(QT):
                    for t in range(QT):
                        last = nc.tensor.transpose(
                            extra[2 + h % 2][:, k * T + t * P:k * T + (t + 1) * P],
                            cross_p[h % 2][:, t * T + k * P:t * T + (k + 1) * P], ident)
                last.then_inc(cross_t, 1)

            for s in range(8):
                if s < 4:
                    job_of(none, JOB_CQ + s, OUT_CQ + s, part_a,
                           (lambda half: (x1_low, 8 + 8 * half)) if s == 0 else None, slot=slot_x1)
                else:
                    if s == 4:
                        pe.wait_ge(taken, BANKS + OUT_CQ + 2)
                    v_job(none, JOB_CQ + s, s - 4, bank[0:2], part_b, mem_low)
                if s == 0:
                    norm_sum(N_X1, extra[3])
                if 1 <= s < 5:
                    cross_scores(s - 1)
                if 3 <= s < 7:
                    cross_turn(s - 3)
            pe.wait_ge(taken, BANKS + OUT_CR)
            for h in range(CROSS):
                pe.wait_ge(cross_wt, h + 1)
                for k in range(QT):
                    last = mm(bank[(h + 2) % 4][:, 0:T], mem_v[:, k, h * P:(h + 1) * P],
                              cross_w[h][:, k * T:(k + 1) * T], start=k == 0, stop=k == QT - 1)
                last.then_inc(cross_o, 1)
            pe.wait_ge(taken, BANKS + OUT_CO)
            short_jobs(JOB_CO, OUT_CO, part_b, 0)
            def up(off, s, ready=None):
                job_of(off, JOB_MLP + s, OUT_MLP + s, part_a, ready)

            def down(q):
                with pe.Fori(0, KT // 4) as i:
                    for s in range(4):
                        off = lambda k: q * (32 * k) + i * (4 * k)
                        job = JOB_MLP + QUARTER + s
                        pe.wait_ge(taken, off(1) + (OUT_MLP + QUARTER + s + 1))
                        for half in range(2):
                            waits = {} if s else {0: 12, 4: 15, 7: 16} if half else {0: 8}
                            waits = {n: q * 16 + (1 + tiles) for n, tiles in waits.items()}
                            half_job(off, job, half, bank[job % 4], part_b, 8 * half,
                                     waits=waits).then_inc(half_done, 1)

            for s in range(4):
                up(none, s, (lambda half: (x2_low, 8 + 8 * half)) if s == 0 else None)
                if s == 0:
                    norm_sum(N_X2, extra[3])
            with pe.Fori(1, QUARTER // 4) as i:
                for s in range(4):
                    up(by(i), s)
            down(0)
            with pe.Fori(1, 4) as q:
                with pe.Fori(0, QUARTER // 4) as i:
                    for s in range(4):
                        up(lambda k: q * (32 * k) + i * (4 * k), s)
                down(q)
            norm_sum(N_LAST, extra[3])


def shape_constants():
    inverse = (1.0 / (np.float32(THETA) ** (np.arange(0, P, 2, dtype=np.float32) / np.float32(P)))).astype(np.float32)
    angle = (np.arange(T, dtype=np.float32)[:, None] * inverse[None, :]).astype(np.float32).T
    cos, sin = np.cos(angle), np.sin(angle)
    rope = np.stack([np.concatenate([cos, cos]), np.concatenate([-sin, sin])], axis=1)

    query, key = np.arange(T)[:, None], np.arange(T)[None, :]
    def tiles(seen):
        bias = np.where(seen, 0.0, NEG).astype(np.float32)
        return np.concatenate([bias[0:P, 0:P], bias[P:T, :]], axis=1)
    causal = tiles(key <= query)
    past = np.where(key < query, 0.0, NEG).astype(np.float32).T
    past = np.concatenate([past[0:P, :], past[P:T, P:T]], axis=1)
    dilated = [tiles((key <= query) & (query - key <= window) & ((query - key) % step == 0))
               for window, step in PATTERNS]
    masks = np.stack([causal, past] + dilated, axis=1)

    row, col = np.arange(P)[:, None], np.arange(P)[None, :]
    square = np.stack([row == col, row >= 0 * col, row >= col], axis=1)
    return (np.ascontiguousarray(rope, dtype=np.float32), np.ascontiguousarray(masks, dtype=np.float32),
            np.ascontiguousarray(square, dtype=np.float32))


def laid_out(inputs):
    a = {k: np.asarray(v) for k, v in inputs.items()}

    def tokens(v):
        return v.T.reshape(KT, P, T).transpose(1, 0, 2)

    def by_output(w):
        k, n = w.shape[0] // P, w.shape[1] // P
        return w.reshape(k, P, n, P).transpose(2, 1, 0, 3).reshape(n, P, k * P)

    def by_512(w):
        return w.reshape(4, 4, P, -1, 512).transpose(3, 0, 2, 1, 4).reshape(-1, P, CHUNK)

    w_in = a["w_in"][0].reshape(D, 3, HEADS, P)
    order = [*range(HEADS_A, HEADS), *range(HEADS_A)]
    q, k = (w_in[:, n][:, order] for n in range(2))
    wqk = np.stack([q, k], axis=2).reshape(D, 2 * HEADS * P)
    w_out = a["w_out"][0]
    ckv = a["w_ckv"][0]

    def by_outputs(w, n):
        return w.reshape(-1, P, KT // n, n, P).transpose(2, 1, 3, 0, 4).reshape(KT // n, P, CHUNK)

    w_down = np.concatenate([by_output(a["w_down"][0][n * D:(n + 1) * D]) for n in range(4)])
    gains = np.concatenate([a["g_mix"][0], a["g_out_b"][0], a["g_out_c"][0], a["g_out_a"][0],
                            a["g_cross"][0], a["g_mem"], a["g_mlp"][0], a["g_final"]]).reshape(GAINS, P).T
    rope, masks, square = shape_constants()
    arrays = {
        "x": tokens(a["x"][0]), "mem": tokens(a["mem"][0]), "wqk": by_output(wqk),
        "wv": by_512(w_in[:, 2].reshape(D, HEADS * P)), "wmk": by_output(ckv[:, :CROSS * P]),
        "wmv": by_512(ckv[:, CROSS * P:]), "wbc": by_outputs(w_out[HEADS_A * P:], 2),
        "woa": by_outputs(w_out[:HEADS_A * P], 4), "wcq": by_output(a["w_cq"][0]),
        "wco": by_outputs(a["w_co"][0], 4), "wup": by_output(a["w_up"][0]), "wdown": w_down, "gains": gains, "rope": rope,
        "masks": masks, "square": square,
    }
    return {f"in_{name}": np.ascontiguousarray(v) for name, v in arrays.items()}


def kernel(**inputs):
    import concourse.bacc as bacc
    from concourse.bass_utils import run_bass_kernel_spmd

    nc = bacc.Bacc("TRN2", target_bir_lowering=False, num_devices=1)
    arrays = laid_out(inputs)
    args = [nc.dram_tensor(name, a.shape, mybir.dt.from_np(a.dtype), kind="ExternalInput").ap()
            for name, a in arrays.items()]
    args.append(nc.dram_tensor("out", (P, KT, T), mybir.dt.float32, kind="ExternalOutput").ap())
    build(nc, *args)
    result = run_bass_kernel_spmd(nc, [arrays], core_ids=[0]).results[0]["out"]
    return np.ascontiguousarray(result.transpose(2, 1, 0).reshape(1, T, D))
```
